# Optimizing a Trainium2 kernel written in Bass

```python
import math
import jax, jax.numpy as jnp
from jax import lax
import numpy as np

D_MODEL = 2048
BATCH = 1
SEQ = 256
DEPTH = 1

MIX_WIDTH = D_MODEL
ATT_WIDTH = MIX_WIDTH // 2
LRU_WIDTH = MIX_WIDTH - ATT_WIDTH
ATT_HEADS = 8
ATT_QK_DIM = ATT_WIDTH // (2 * ATT_HEADS)
ATT_V_DIM = ATT_WIDTH // ATT_HEADS
LRU_HEADS = 8
LRU_BLOCK = LRU_WIDTH // LRU_HEADS
CONV_WIDTH = 4
LRU_C = 8.0
Q_BLOCK = 128
IN_WIDTH = 3 * ATT_WIDTH + 2 * LRU_WIDTH
PEER_HEADS = 8
PEER_KEYS = 128
PEER_EXPERTS = PEER_KEYS * PEER_KEYS
PEER_QDIM = 256
PEER_HALF = PEER_QDIM // 2
PEER_TOPK = 16
PEER_CHUNK = 128
DN_ALPHA = (2.0 * DEPTH) ** 0.25
DN_BETA = (8.0 * DEPTH) ** -0.25
LN_EPS = 1e-5

kernel_name = 'hybrid_diffattn_rglru_peer'

def layer_norm(x, g, b):
    xf = x.astype(jnp.float32)
    mu = jnp.mean(xf, axis=-1, keepdims=True)
    var = jnp.mean(jnp.square(xf - mu), axis=-1, keepdims=True)
    return ((xf - mu) * lax.rsqrt(var + LN_EPS) * g + b).astype(x.dtype)

def rms_norm(x, g):
    xf = x.astype(jnp.float32)
    return xf * lax.rsqrt(jnp.mean(jnp.square(xf), axis=-1, keepdims=True) + LN_EPS) * g

def alibi_slopes():
    return jnp.exp2(-8.0 * jnp.arange(1, ATT_HEADS + 1, dtype=jnp.float32) / ATT_HEADS)

def diff_attention(q, k, v, lam, subln_g, lambda_init):
    B, S, _ = q.shape
    q = q.astype(jnp.float32).reshape(B, S, ATT_HEADS, 2, ATT_QK_DIM).transpose(0, 2, 3, 1, 4)
    k = k.astype(jnp.float32).reshape(B, S, ATT_HEADS, 2, ATT_QK_DIM).transpose(0, 2, 3, 1, 4)
    v = v.astype(jnp.float32).reshape(B, S, ATT_HEADS, ATT_V_DIM).transpose(0, 2, 1, 3)
    scale = ATT_QK_DIM ** -0.5
    slopes = alibi_slopes()
    key_pos = jnp.arange(S)

    def attend_block(i):
        start = i * Q_BLOCK
        qb = lax.dynamic_slice_in_dim(q, start, Q_BLOCK, axis=3)
        s = jnp.einsum('bhcqd,bhckd->bhcqk', qb, k) * scale
        dist = (start + jnp.arange(Q_BLOCK))[:, None] - key_pos[None, :]
        s = s - (slopes[:, None, None] * dist)[None, :, None]
        s = jnp.where(dist >= 0, s, -jnp.inf)
        p = jax.nn.softmax(s, axis=-1)
        pd = p[:, :, 0] - lam * p[:, :, 1]
        return jnp.einsum('bhqk,bhkd->bhqd', pd, v)

    o = lax.map(attend_block, jnp.arange(S // Q_BLOCK))
    o = o.transpose(1, 0, 3, 2, 4).reshape(B, S, ATT_HEADS, ATT_V_DIM)
    o = rms_norm(o, subln_g) * (1.0 - lambda_init)
    return o.reshape(B, S, ATT_WIDTH)

def causal_dwconv(x, w, b):
    S = x.shape[1]
    xp = jnp.pad(x, ((0, 0), (CONV_WIDTH - 1, 0), (0, 0)))
    y = xp[:, 0:S] * w[0]
    for j in range(1, CONV_WIDTH):
        y = y + xp[:, j:j + S] * w[j]
    return y + b

def rg_lru(xc, w_a, b_a, w_x, b_x, lam):
    B, S, _ = xc.shape
    xf = xc.astype(jnp.float32)
    xh = xf.reshape(B, S, LRU_HEADS, LRU_BLOCK)
    r = jax.nn.sigmoid(jnp.einsum('bshi,hij->bshj', xh, w_a.astype(jnp.float32)) + b_a).reshape(B, S, LRU_WIDTH)
    ig = jax.nn.sigmoid(jnp.einsum('bshi,hij->bshj', xh, w_x.astype(jnp.float32)) + b_x).reshape(B, S, LRU_WIDTH)
    log_a = -LRU_C * r * jax.nn.softplus(-lam.astype(jnp.float32))
    a = jnp.exp(log_a)
    bt = jnp.sqrt(-jnp.expm1(2.0 * log_a)) * (ig * xf)

    def combine(left, right):
        a_l, b_l = left
        a_r, b_r = right
        return a_l * a_r, a_r * b_l + b_r

    _, h = lax.associative_scan(combine, (a, bt), axis=1)
    return h.astype(xc.dtype)

def peer_ffn(x, wq, subkeys, u_tab, v_tab):
    B, S, D = x.shape
    xt = x.reshape((B * S) // PEER_CHUNK, PEER_CHUNK, D)
    K = PEER_TOPK

    def chunk(xc):
        C = xc.shape[0]
        q = (xc @ wq).astype(jnp.float32).reshape(C, PEER_HEADS, 2, PEER_HALF)
        sc = jnp.einsum('chpd,hpnd->chpn', q, subkeys.astype(jnp.float32))
        s_half, i_half = lax.top_k(sc, K)
        cand = s_half[:, :, 0, :, None] + s_half[:, :, 1, None, :]
        s_top, j = lax.top_k(cand.reshape(C, PEER_HEADS, K * K), K)
        ia = j // K
        ib = j % K
        e = (jnp.take_along_axis(i_half[:, :, 0], ia, axis=-1) * PEER_KEYS
             + jnp.take_along_axis(i_half[:, :, 1], ib, axis=-1))
        g = jax.nn.softmax(s_top, axis=-1)
        u = u_tab[e]
        hid = jax.nn.gelu(jnp.einsum('chkd,cd->chk', u, xc).astype(jnp.float32))
        w = (g * hid).astype(xc.dtype)
        return jnp.einsum('chk,chkd->cd', w, v_tab[e])

    return lax.map(chunk, xt).reshape(B, S, D)

def setup_inputs(seed: int = 0) -> dict:
    key = jax.random.key(seed)
    ks = jax.random.split(key, 24)
    f32 = jnp.float32
    nrm = lambda k, shape, s: jax.random.normal(k, shape, f32) * s
    x = nrm(ks[0], (BATCH, SEQ, D_MODEL), 1.0)
    col_scale = jnp.concatenate([jnp.ones((2 * ATT_WIDTH,), f32),
                                 jnp.full((ATT_WIDTH + 2 * LRU_WIDTH,), DN_BETA, f32)])
    w_in = nrm(ks[1], (DEPTH, D_MODEL, IN_WIDTH), D_MODEL ** -0.5) * col_scale
    conv_w = nrm(ks[2], (DEPTH, CONV_WIDTH, LRU_WIDTH), CONV_WIDTH ** -0.5)
    conv_b = nrm(ks[3], (DEPTH, LRU_WIDTH), 0.01)
    w_rg_a = nrm(ks[4], (DEPTH, LRU_HEADS, LRU_BLOCK, LRU_BLOCK), LRU_BLOCK ** -0.5)
    b_rg_a = nrm(ks[5], (DEPTH, LRU_HEADS, LRU_BLOCK), 0.01)
    w_rg_x = nrm(ks[6], (DEPTH, LRU_HEADS, LRU_BLOCK, LRU_BLOCK), LRU_BLOCK ** -0.5)
    b_rg_x = nrm(ks[7], (DEPTH, LRU_HEADS, LRU_BLOCK), 0.01)
    u = jax.random.uniform(ks[8], (DEPTH, LRU_WIDTH), f32, minval=0.9, maxval=0.999)
    p = u ** (1.0 / LRU_C)
    lru_lambda = jnp.log(p) - jnp.log1p(-p)
    lambda_q1 = nrm(ks[9], (DEPTH, ATT_QK_DIM), 0.1)
    lambda_k1 = nrm(ks[10], (DEPTH, ATT_QK_DIM), 0.1)
    lambda_q2 = nrm(ks[11], (DEPTH, ATT_QK_DIM), 0.1)
    lambda_k2 = nrm(ks[12], (DEPTH, ATT_QK_DIM), 0.1)
    subln_g = 1.0 + nrm(ks[13], (DEPTH, ATT_V_DIM), 0.01)
    w_out = nrm(ks[14], (DEPTH, MIX_WIDTH, D_MODEL), MIX_WIDTH ** -0.5 * DN_BETA)
    ln1_g = 1.0 + nrm(ks[15], (DEPTH, D_MODEL), 0.01)
    ln1_b = nrm(ks[16], (DEPTH, D_MODEL), 0.01)
    peer_wq = nrm(ks[17], (DEPTH, D_MODEL, PEER_HEADS * PEER_QDIM), D_MODEL ** -0.5)
    peer_subkeys = nrm(ks[18], (DEPTH, PEER_HEADS, 2, PEER_KEYS, PEER_HALF), PEER_HALF ** -0.5)
    peer_u = nrm(ks[19], (DEPTH, PEER_EXPERTS, D_MODEL), D_MODEL ** -0.5 * DN_BETA)
    peer_v = nrm(ks[20], (DEPTH, PEER_EXPERTS, D_MODEL), DN_BETA)
    ln2_g = 1.0 + nrm(ks[21], (DEPTH, D_MODEL), 0.01)
    ln2_b = nrm(ks[22], (DEPTH, D_MODEL), 0.01)
    return {'x': x, 'w_in': w_in, 'conv_w': conv_w, 'conv_b': conv_b,
            'w_rg_a': w_rg_a, 'b_rg_a': b_rg_a, 'w_rg_x': w_rg_x, 'b_rg_x': b_rg_x,
            'lru_lambda': lru_lambda, 'lambda_q1': lambda_q1, 'lambda_k1': lambda_k1,
            'lambda_q2': lambda_q2, 'lambda_k2': lambda_k2, 'subln_g': subln_g,
            'w_out': w_out, 'ln1_g': ln1_g, 'ln1_b': ln1_b, 'peer_wq': peer_wq,
            'peer_subkeys': peer_subkeys, 'peer_u': peer_u, 'peer_v': peer_v,
            'ln2_g': ln2_g, 'ln2_b': ln2_b}

def reference(x, w_in, conv_w, conv_b, w_rg_a, b_rg_a, w_rg_x, b_rg_x, lru_lambda,
              lambda_q1, lambda_k1, lambda_q2, lambda_k2, subln_g, w_out, ln1_g, ln1_b,
              peer_wq, peer_subkeys, peer_u, peer_v, ln2_g, ln2_b):
    h = x
    splits = [ATT_WIDTH, 2 * ATT_WIDTH, 3 * ATT_WIDTH, 3 * ATT_WIDTH + LRU_WIDTH]
    for l in range(DEPTH):
        proj = h @ w_in[l]
        q, k, v, xr, xg = jnp.split(proj, splits, axis=-1)
        lambda_init = 0.8 - 0.6 * math.exp(-0.3 * l)
        lam = (jnp.exp(jnp.sum(lambda_q1[l].astype(jnp.float32) * lambda_k1[l].astype(jnp.float32)))
               - jnp.exp(jnp.sum(lambda_q2[l].astype(jnp.float32) * lambda_k2[l].astype(jnp.float32)))
               + lambda_init)
        att = diff_attention(q, k, v, lam, subln_g[l], lambda_init).astype(h.dtype)
        xc = causal_dwconv(xr, conv_w[l], conv_b[l])
        lru = rg_lru(xc, w_rg_a[l], b_rg_a[l], w_rg_x[l], b_rg_x[l], lru_lambda[l]) * jax.nn.gelu(xg)
        mix = jnp.concatenate([att, lru], axis=-1) @ w_out[l]
        h = layer_norm(DN_ALPHA * h + mix, ln1_g[l], ln1_b[l])
        ffn = peer_ffn(h, peer_wq[l], peer_subkeys[l], peer_u[l], peer_v[l])
        h = layer_norm(DN_ALPHA * h + ffn, ln2_g[l], ln2_b[l])
    return h


_drawn_inputs = setup_inputs


def setup_inputs(seed=0):
    import zlib

    import numpy as np

    out = dict(_drawn_inputs(seed))
    spreads = {}
    factors = {'conv_b': 45.744,
     'w_rg_a': 33.208,
     'b_rg_a': 64.0,
     'w_rg_x': 22.744,
     'b_rg_x': 64.0,
     'lru_lambda': 25.944,
     'lambda_q1': 5.615,
     'lambda_k1': 8.0,
     'subln_g': 33.07,
     'ln1_g': 12.546,
     'ln1_b': 13.7,
     'ln2_g': 30.315,
     'ln2_b': 31.184,
     'conv_w': 8.0,
     'lambda_q2': 8.0,
     'lambda_k2': 8.0}
    for name, (base, spread) in spreads.items():
        noise = np.random.default_rng([zlib.crc32(name.encode()), seed]).standard_normal(out[name].shape)
        drawn = base * np.exp(spread * noise) if base else spread * noise
        out[name] = __import__('jax').numpy.asarray(drawn.astype(out[name].dtype))
    for name, factor in factors.items():
        out[name] = (out[name] * factor).astype(out[name].dtype)
    return out
```

```python
import math

import numpy as np

import concourse.bass as bass
from concourse import mybir
from contextlib import ExitStack


def hybrid_layer(nc, xT, x, w_in, w_out, w_q, uT, v_tab, subkeysT, params, lambdas, subln_g, w_rg,
                 ln1_g, ln1_b, ln2_g, ln2_b, out, gelu_dram, h_dram):
    f32, f32r, u32 = mybir.dt.float32, mybir.dt.float32r, mybir.dt.uint32
    ALU, ACT, AX = mybir.AluOpType, mybir.ActivationFunctionType, mybir.AxisListType

    P = 128
    D_MODEL = 2048
    SEQ = 256
    TILES = SEQ // P
    KC = D_MODEL // P
    COLS = 512
    SLABS = 4
    HEADS = 8
    QK_DIM = 64
    TOPK = 16
    LRU_CHUNKS = 8
    PAD = 3
    XROW = SEQ + PAD
    ALPHA = 2.0 ** 0.25
    EPS = 1e-5
    LAMBDA_INIT = 0.8 - 0.6 * math.exp(0.0)
    MASKED = -1e30
    LOWEST = -3.0e38

    IN0, OUT0, WQ0, U0, V0 = 0, 10, 14, 18, 50
    NB_IN, NB_OUT, NB_WQ, NB_U, NB_V = 10, 4, 4, 32, 32
    ROUTE = TILES * HEADS

    ctx = ExitStack()
    with ctx:
        def sb(name, shape, dt=f32, stack=ctx):
            return stack.enter_context(nc.sbuf_tensor(name, shape, dt))

        def sem(name):
            return ctx.enter_context(nc.semaphore(name))

        raw = sb("raw", [P, SLABS, 2048])
        hi = sb("slab_hi", [P, 2, 4, COLS], f32r)
        lo = sb("slab_lo", [P, 2, 4, COLS], f32r)
        stage = sb("stage", [P, 2048])
        small = sb("small", [P, 768])
        picks_scope = ExitStack()
        picks = sb("picks", [P, 3, SEQ], stack=picks_scope)
        iota = sb("iota", [P, P], stack=picks_scope)
        picks_scope.close()
        wT_hi = sb("wT_hi", [P, 2, SEQ], f32r)
        wT_lo = sb("wT_lo", [P, 2, SEQ], f32r)
        front = ExitStack()
        aT_hi = sb("aT_hi", [P, KC, SEQ], f32r, front)
        aT_lo = sb("aT_lo", [P, KC, SEQ], f32r, front)
        arena = sb("arena", [P, 24576], f32, front)
        front.close()
        gates = sb("gates", [P, P, SEQ])
        ps = ctx.enter_context(nc.psum_tensor("ps", [P, 8, COLS], f32))

        def at(off, *dims):
            n = int(np.prod(dims))
            v = arena[:, off:off + n]
            if len(dims) == 1:
                return v
            names = "abcd"[:len(dims)]
            return v.rearrange(f"p ({' '.join(names)}) -> p {' '.join(names)}",
                               **{k: d for k, d in zip(names, dims)})

        xs = at(0, KC, SEQ)
        proj = at(4096, NB_IN, TILES, COLS)
        qT, kT = at(14336, HEADS, SEQ), at(16384, HEADS, SEQ)
        xgT = at(18432, LRU_CHUNKS, SEQ)
        xrT = at(8192, LRU_CHUNKS, XROW)
        xc, th = at(0, LRU_CHUNKS, SEQ), at(2048, LRU_CHUNKS, SEQ)
        ig, rc = at(4096, LRU_CHUNKS, SEQ), at(6144, LRU_CHUNKS, SEQ)
        sq = at(8192, LRU_CHUNKS, SEQ)
        att = at(20480, TILES, HEADS, P)
        dist = at(22528, 384)
        sx = at(10272, 2, 2, 384)
        pdT = at(22912, 2, 3, P)
        par = at(23680, 64)
        lamv = at(23744, 4, QK_DIM)
        subg = at(24000, P)
        st = at(24128, 320)
        ident = at(24448, P)
        xn = at(14336, TILES, D_MODEL)
        z = at(4096, TILES, D_MODEL)
        lng, lnb = at(8192, D_MODEL), at(10240, D_MODEL)
        pq = at(0, NB_WQ, TILES, COLS)
        pqT = at(8192, 2 * HEADS, SEQ)
        skT = at(12288, 2 * HEADS, P)
        sc = at(14336, TILES, 2 * HEADS * P)
        sc_flat = at(14336, TILES * 2 * HEADS * P)
        gs = at(0, TILES, COLS)

        conv_w = lambda j, c: par[:, 8 * j + c:8 * j + c + 1]
        conv_b = lambda c: par[:, 32 + c:33 + c]
        b_a = lambda c: par[:, 40 + c:41 + c]
        b_x = lambda c: par[:, 48 + c:49 + c]

        rg_a = lambda c: stage[:, P * c:P * (c + 1)]
        rg_x = lambda c: stage[:, 1024 + P * c:1024 + P * (c + 1)]
        hT = stage[:, 0:1024].rearrange("p (c t) -> p c t", t=SEQ)
        onehot = stage[:, :].rearrange("p (s w t k) -> p s w t k", s=2, w=2, t=4)

        gflat = gates[:, :, :].rearrange("p a b -> p (a b)")

        def gates_z(i):
            return gflat[:, 8192 + i * D_MODEL:8192 + (i + 1) * D_MODEL]

        h_back = gflat[:, 0:4096].rearrange("p (i d) -> p i d", d=D_MODEL)
        lng2, lnb2 = gflat[:, 4096:6144], gflat[:, 6144:8192]

        def ps4(bank):
            return ps[:, bank, :].rearrange("p (c t) -> p c t", t=SEQ)

        def front_target(n):
            kind, c = n // 4, 2 * (n % 4)
            if kind == 2:
                return xrT[:, c:c + 2, PAD:]
            return (qT, kT, None, xgT)[kind][:, c:c + 2, :]

        def sc_bank(n):
            return sc[:, n // 4, (n % 4) * 512:(n % 4 + 1) * 512]

        def w_f(s):
            return small[:, 256 + (s % 2) * SEQ:256 + (s % 2 + 1) * SEQ]

        scu = at(18432, 2, P)
        rep = at(18688, 2, P)
        cand, crep = at(18944, 256), at(19200, 256)
        cmp = at(19456, 2, TOPK, TOPK)
        m32 = at(19968, 2, TOPK)
        ix = at(20000, 2, TOPK).bitcast(u32)
        ixf = at(20032, 2, TOPK)
        top, topix = at(20064, TOPK), at(20080, TOPK).bitcast(u32)
        ab = at(20096, 2, TOPK).bitcast(u32)
        abf = at(20128, 2, TOPK)
        gate_exp = at(20480, ROUTE, TOPK)
        key_a = at(20736, ROUTE, TOPK)
        key_b = at(20992, ROUTE, TOPK)
        gsum = at(21248, ROUTE)
        logits = at(19456, ROUTE, TOPK)

        def stat(i, base, a, n=1):
            o = 128 * (base // 2) + 64 * i + a
            return small[:, o:o + n]

        def norm_scalar(act, base):
            for i in range(TILES):
                act.wait_ge(s_var, base + i + 1)
                act.activation(stat(i, base, 27), stat(i, base, 26), ACT.Sqrt).then_inc(s_std, 1)
            for i in range(TILES):
                zt = z[:, i, :] if base == 0 else gates_z(i)
                act.wait_ge(s_nb, base + i + 1)
                act.activation(zt, zt, ACT.Identity, bias=stat(i, base, 30),
                               scale=stat(i, base, 29)).then_inc(s_nrm, 1)

        loaded = [sem(f"slab_loaded_{s}") for s in range(SLABS)]
        hi_ready, lo_ready, slab_used = sem("hi_ready"), sem("lo_ready"), sem("slab_used")
        banks_free = sem("banks_free")
        s_const, s_par, s_xs = sem("const_ready"), sem("params_loaded"), sem("xT_loaded")
        s_xhi, s_xlo = sem("x_hi_ready"), sem("x_lo_ready")
        s_tr = sem("front_transposed")
        s_trc, s_qtc, s_scc = ([sem(f"{n}_by_{e}") for e in ("act", "dve")]
                               for n in ("front_transposes_taken", "q_transposes_taken", "key_scores_taken"))
        s_cp = sem("conv_done")
        s_gate, s_sig = sem("lru_gates_in_psum"), sem("lru_sigmoid_done")
        s_tanh, s_sp, s_u, s_t2, s_sq = (sem("lru_tanh_done"), sem("lru_rate_ready"), sem("lru_exp_done"),
                                         sem("lru_tanh_clamped"), sem("lru_sqrt_done"))
        s_gx, s_lru, s_lruhi = sem("xg_gelu_done"), sem("lru_done"), sem("lru_hi_ready")
        s_lexp, s_lsum = sem("lambda_exp_done"), sem("lambda_sums_ready")
        s_sc, s_sx, s_e, s_pd = sem("scores_in_psum"), sem("scores_biased"), sem("exp_done"), sem("probs_ready")
        s_pt, s_ptc, s_o, s_oc = sem("probs_transposed"), sem("probs_transposes_taken"), sem("att_in_psum"), sem("att_taken")
        s_ms, s_rt, s_attn = sem("att_mean_square"), sem("att_root"), sem("att_normed")
        s_mt, s_mhi, s_mlo = sem("mix_transposed"), sem("mix_hi_ready"), sem("mix_lo_ready")
        s_xn, s_ln1w, s_z = sem("x_loaded"), sem("ln1_weights_loaded"), sem("residual_ready")
        s_var, s_std, s_nb, s_nrm = sem("variance_ready"), sem("std_ready"), sem("norm_bias_ready"), sem("normed")
        s_h, s_hst = sem("h_ready"), sem("h_stored")
        s_sk = sem("subkeys_loaded")
        s_qt, s_scp = sem("q_transposed"), sem("key_scores_in_psum")
        s_gelu, s_ht, s_htc, s_hts = sem("gelu_done"), sem("gelu_transposed"), sem("gelu_transposes_taken"), sem("gelu_stored")
        s_route, s_pass = sem("route_chain"), sem("route_passed")
        s_gm, s_ge, s_gt = sem("gate_logits_ready"), sem("gate_exp_done"), sem("gates_ready")
        s_pk, s_pkc = sem("picks_transposed"), sem("picks_ready")
        s_iota, s_rg = sem("iota_ready"), sem("lru_gate_weights_loaded")
        s_oh, s_G, s_Gc = sem("onehots_ready"), sem("gates_in_psum"), sem("gates_taken")
        s_hin = [sem("gelu_loaded_0"), sem("gelu_loaded_1")]
        s_w, s_whi, s_wlo = sem("w_ready"), sem("w_hi_ready"), sem("w_lo_ready")
        s_hre, s_ln2w, s_z2 = sem("h_reloaded"), sem("ln2_weights_loaded"), sem("residual2_ready")
        s_y, s_out = sem("y_ready"), sem("out_stored")
        s_dv = sem("vector_chain")

        block = ctx.enter_context(nc.Block())

        def newton(dv, link, root, var, tmp):
            link(dv.reciprocal(root, root))
            link(dv.tensor_tensor(tmp, root, root, ALU.mult))
            link(dv.tensor_tensor(tmp, tmp, var, ALU.mult))
            link(dv.tensor_scalar(tmp, tmp, -0.5, 1.5, ALU.mult, ALU.add))
            link(dv.tensor_tensor(root, root, tmp, ALU.mult))

        def norm_vector(dv, link, base, g, b, ready):
            for i in range(TILES):
                zt = z[:, i, :] if base == 0 else gates_z(i)
                for k in range(4):
                    last = dv.bn_stats(stat(i, base, 6 * k, 6), zt[:, COLS * k:COLS * (k + 1)])
                link(last)
                link(dv.bn_aggr(stat(i, base, 24, 2), stat(i, base, 0, 24)))
                dv.tensor_scalar(stat(i, base, 26), stat(i, base, 25), EPS, None, ALU.add).then_inc(s_var, 1)
            for i in range(TILES):
                dv.wait_ge(s_std, base + i + 1)
                link(dv.tensor_scalar(stat(i, base, 29), stat(i, base, 27), 1.0, None, ALU.mult))
                newton(dv, link, stat(i, base, 29), stat(i, base, 26), stat(i, base, 28))
                dv.tensor_scalar(stat(i, base, 30), stat(i, base, 24), stat(i, base, 29), -1.0,
                                 ALU.mult, ALU.mult).then_inc(s_nb, 1)
            for i in range(TILES):
                zt = z[:, i, :] if base == 0 else gates_z(i)
                dv.wait_ge(s_nrm, base + i + 1)
                link(dv.tensor_tensor(zt, zt, g, ALU.mult))
                dv.tensor_tensor(zt, zt, b, ALU.add).then_inc(ready, 1)

        @block.sync
        def _(sp):
            def stream(src, blocks, base, first=0):
                with sp.Fori(first, blocks) as b:
                    for s in range(SLABS):
                        sp.wait_ge(lo_ready, 4 * b + (4 * base + s - 3))
                        sp.dma_start(raw[:, s, :], src[b, s]).then_inc(loaded[s], 16)

            for s in range(SLABS):
                sp.dma_start(raw[:, s, :], w_in[0, s]).then_inc(loaded[s], 16)
            stream(w_in, NB_IN, IN0, first=1)
            stream(w_out, NB_OUT, OUT0)
            stream(w_q, NB_WQ, WQ0)
            stream(uT, NB_U, U0)
            stream(v_tab, NB_V, V0)
            out_v = out.rearrange("b (i p) d -> p (b i) d", p=P)
            for i in range(TILES):
                sp.wait_ge(s_y, i + 1)
                sp.dma_start(out_v[:, i, :], gates_z(i)).then_inc(s_out, 16)
            sp.wait_ge(s_out, 16 * TILES)

        @block.gpsimd
        def _(pool):
            pool.dma_start(xs, xT).then_inc(s_xs, 16)
            pool.memset(ident, 0.0).then_inc(s_const, 1)
            pool.dma_start(stage[:, :].rearrange("p (w h j) -> p w h j", w=2, h=LRU_CHUNKS), w_rg).then_inc(s_rg, 16)
            pool.iota(dist[:, 0:128], [[1, 128]], base=0, channel_multiplier=-1,
                      allow_small_or_imprecise_dtypes=True).then_inc(s_const, 1)
            pool.iota(dist[:, 128:384], [[1, 256]], base=-P, channel_multiplier=-1,
                      allow_small_or_imprecise_dtypes=True).then_inc(s_const, 1)
            pool.iota(iota[:, :], [[1, P]], base=0, channel_multiplier=0,
                      allow_small_or_imprecise_dtypes=True).then_inc(s_iota, 1)
            pool.wait_ge(s_const, 3)
            pool.affine_select(out=ident, in_=ident, compare_op=ALU.not_equal, fill=1.0, base=0,
                               pattern=[[-1, P]], channel_multiplier=1).then_inc(s_const, 1)
            pool.affine_select(out=dist[:, 0:128], in_=dist[:, 0:128], compare_op=ALU.is_ge, fill=MASKED,
                               base=0, pattern=[[-1, 128]], channel_multiplier=1).then_inc(s_const, 1)
            pool.affine_select(out=dist[:, 128:384], in_=dist[:, 128:384], compare_op=ALU.is_ge, fill=MASKED,
                               base=P, pattern=[[-1, 256]], channel_multiplier=1).then_inc(s_const, 1)
            pool.dma_start(par, params).then_inc(s_par, 16)
            pool.dma_start(lamv, lambdas.partition_broadcast(P)).then_inc(s_par, 16)
            pool.dma_start(subg, subln_g.partition_broadcast(P)).then_inc(s_par, 16)
            pool.wait_ge(s_attn, 1)
            pool.dma_start(xn, x.rearrange("(i p) d -> p i d", p=P)).then_inc(s_xn, 16)
            pool.wait_ge(s_lru, 1)
            pool.dma_start(lng, ln1_g.partition_broadcast(P)).then_inc(s_ln1w, 16)
            pool.dma_start(lnb, ln1_b.partition_broadcast(P)).then_inc(s_ln1w, 16)
            pool.dma_start(skT, subkeysT).then_inc(s_sk, 16)
            pool.wait_ge(s_h, 2)
            pool.dma_start(h_dram.rearrange("(i p) d -> p i d", p=P), z).then_inc(s_hst, 16)
            pool.wait_ge(s_hst, 16)
            pool.wait_ge(s_htc, 2)
            pool.dma_start(gelu_dram[0], hT).then_inc(s_hts, 16)
            with pool.Fori(1, NB_U) as j:
                pool.wait_ge(s_htc, j + 2)
                pool.dma_start(gelu_dram[j], hT).then_inc(s_hts, 16)
            pool.wait_ge(s_hts, 16 * NB_U)
            pool.wait_ge(s_G, 64)
            for half in range(2):
                pool.dma_start(hT[:, 2 * half:2 * half + 2, :], gelu_dram[0, :, 2 * half:2 * half + 2, :])\
                    .then_inc(s_hin[half], 16)
            with pool.Fori(1, NB_V) as b:
                for half in range(2):
                    pool.wait_ge(s_w, 4 * b + (2 * half - 2))
                    pool.dma_start(hT[:, 2 * half:2 * half + 2, :], gelu_dram[b, :, 2 * half:2 * half + 2, :])\
                        .then_inc(s_hin[half], 16)
            pool.dma_start(h_back, h_dram.rearrange("(i p) d -> p i d", p=P)).then_inc(s_hre, 16)
            pool.dma_start(lng2, ln2_g.partition_broadcast(P)).then_inc(s_ln2w, 16)
            pool.dma_start(lnb2, ln2_b.partition_broadcast(P)).then_inc(s_ln2w, 16)

        @block.scalar
        def _(act):
            def split_hi(B, s, reused=True):
                act.wait_ge(loaded[s], 16 * B + 16)
                if reused:
                    act.wait_ge(slab_used, 4 * B + (s - 1))
                act.activation(hi[:, s % 2], raw[:, s, :].rearrange("p (c n) -> p c n", n=COLS),
                               ACT.Copy).then_inc(hi_ready, 1)

            def pair(par_):
                return ps[:, bass.ds(par_ * 2, 2), :]

            act.wait_ge(s_xs, 16)
            act.activation(aT_hi[:, :, :], xs, ACT.Copy).then_inc(s_xhi, 1)
            for s in range(SLABS):
                split_hi(IN0, s, reused=s >= 2)

            def take_proj(b):
                act.wait_ge(slab_used, 4 * b + 4)
                act.activation(proj_block(b), pair(b % 2), ACT.Copy).then_inc(banks_free, 1)

            def proj_block(b):
                return arena[:, bass.ds(4096 + b * (TILES * COLS), TILES * COLS)]\
                    .rearrange("p (i n) -> p i n", n=COLS)

            with act.Fori(1, NB_IN) as b:
                split_hi(b, 0)
                split_hi(b, 1)
                take_proj(b - 1)
                split_hi(b, 2)
                split_hi(b, 3)
            take_proj(NB_IN - 1)

            act.wait_ge(s_sp, 1)
            act.activation(st[:, 8:16], st[:, 0:8], ACT.Exp).then_inc(s_u, 1)
            act.wait_ge(s_lsum, 1)
            act.activation(st[:, 130:132], st[:, 128:130], ACT.Exp).then_inc(s_lexp, 1)
            for n in range(16):
                if n % 2 == 0:
                    act.wait_ge(s_tr, n + 1)
                    act.activation(front_target(n), ps4(4 + n % 4), ACT.Copy).then_inc(s_trc[0], 1)

            for c in range(LRU_CHUNKS):
                act.wait_ge(s_gate, c + 1)
                act.activation(th[:, c, :], ps[:, 4 + c % 4, 0:SEQ], ACT.Sigmoid, bias=b_a(c)).then_inc(s_sig, 1)
                act.activation(ig[:, c, :], ps[:, 4 + c % 4, SEQ:2 * SEQ], ACT.Sigmoid, bias=b_x(c)).then_inc(s_sig, 1)
            act.wait_ge(s_sig, 16)
            act.wait_ge(s_sp, 2)
            for c in range(LRU_CHUNKS):
                act.activation(th[:, c, :], th[:, c, :], ACT.Tanh, scale=st[:, 16 + c:17 + c]).then_inc(s_tanh, 1)
            act.wait_ge(s_trc[1], 8)
            act.wait_ge(s_trc[0], 8)
            act.activation(xgT, xgT, ACT.Gelu_apprx_tanh).then_inc(s_gx, 1)
            act.wait_ge(s_t2, 1)
            act.activation(sq, sq, ACT.Sqrt).then_inc(s_sq, 1)

            def exps(h):
                act.wait_ge(s_sx, h + 1)
                mx = st[:, 32 + 4 * (h % 2):36 + 4 * (h % 2)]
                sm = st[:, 40 + 4 * (h % 2):44 + 4 * (h % 2)]
                for c in range(2):
                    for i in range(2):
                        keys = slice(0, 128) if i == 0 else slice(128, 384)
                        act.activation(sx[:, h % 2, c, keys], sx[:, h % 2, c, keys], ACT.Exp,
                                       bias=mx[:, 2 * c + i:2 * c + i + 1], scale=0.125,
                                       accum_out=sm[:, 2 * c + i:2 * c + i + 1]).then_inc(s_e, 1)

            def take_head(h):
                act.wait_ge(s_pt, h + 1)
                act.activation(pdT[:, h % 2], ps[:, h % 2, 0:384].rearrange("p (a k) -> p a k", k=P),
                               ACT.Copy).then_inc(s_ptc, 1)
                act.wait_ge(s_o, h + 1)
                act.activation(att[:, :, h, :], ps[:, 2 + h % 2, 0:256].rearrange("p (i d) -> p i d", d=P),
                               ACT.Copy).then_inc(s_oc, 1)

            for h in range(HEADS + 1):
                if h < HEADS:
                    exps(h)
                if h >= 1:
                    take_head(h - 1)
            act.wait_ge(s_ms, 1)
            act.activation(st[:, 64:80], st[:, 48:64], ACT.Sqrt).then_inc(s_rt, 1)

            act.wait_ge(s_lru, 1)
            act.activation(aT_hi[:, 8:16, :], xc, ACT.Copy).then_inc(s_lruhi, 1)
            for n in range(4):
                act.wait_ge(s_mt, n + 1)
                act.activation(aT_hi[:, 2 * n:2 * n + 2, :], ps4(4 + n), ACT.Copy).then_inc(s_mhi, 1)

            with act.Fori(OUT0, OUT0 + NB_OUT) as B:
                for s in range(SLABS):
                    split_hi(B, s)
            split_hi(WQ0, 0)

            norm_scalar(act, 0)

            for n in range(8):
                act.wait_ge(s_mt, 5 + n)
                act.activation(aT_hi[:, 2 * n:2 * n + 2, :], ps4(4 + n % 4), ACT.Copy).then_inc(s_mhi, 1)

            def take_pq(b):
                act.wait_ge(slab_used, 4 * (WQ0 + 1) + 4 * b)
                act.activation(arena[:, bass.ds(b * (TILES * COLS), TILES * COLS)]
                               .rearrange("p (i n) -> p i n", n=COLS), pair(b % 2), ACT.Copy).then_inc(banks_free, 1)

            for s in range(1, SLABS):
                split_hi(WQ0, s)
            with act.Fori(1, NB_WQ) as b:
                split_hi(b + WQ0, 0)
                split_hi(b + WQ0, 1)
                take_pq(b - 1)
                split_hi(b + WQ0, 2)
                split_hi(b + WQ0, 3)
            take_pq(NB_WQ - 1)
            for n in range(8):
                if n % 2 == 0:
                    act.wait_ge(s_qt, n + 1)
                    act.activation(pqT[:, 2 * n:2 * n + 2, :], ps4(4 + n % 4), ACT.Copy).then_inc(s_qtc[0], 1)
            for n in range(8):
                if n % 2 == 0:
                    act.wait_ge(s_scp, n + 1)
                    act.activation(sc_bank(n), ps[:, n % 4, :], ACT.Copy).then_inc(s_scc[0], 1)

            def gelu(j):
                act.wait_ge(slab_used, 4 * (U0 + 1) + 4 * j)
                act.activation(gs, pair(j % 2), ACT.Gelu_apprx_tanh).then_inc(banks_free, 1)
            for s in range(SLABS):
                split_hi(U0, s)

            def u_block(j):
                split_hi(j + U0, 0)
                split_hi(j + U0, 1)
                gelu(j - 1)
                split_hi(j + U0, 2)
                split_hi(j + U0, 3)
            with act.Fori(1, ROUTE) as j:
                u_block(j)
            act.wait_ge(s_gm, 1)
            act.activation(gate_exp, gate_exp, ACT.Exp).then_inc(s_ge, 1)
            with act.Fori(ROUTE, NB_U) as j:
                u_block(j)
            gelu(NB_U - 1)

            for s in range(2):
                split_hi(V0, s)

            def take_gates(t0, slot, n):
                act.wait_ge(s_G, n)
                act.activation(gates[:, :, bass.ds(t0, 4)].rearrange("p i t -> p t i"),
                               ps[:, slot, :].rearrange("p (t i) -> p t i", i=P), ACT.Copy).then_inc(s_Gc, 1)

            with act.Fori(0, SEQ // 8) as g:
                for slot in range(2):
                    take_gates(8 * g + 4 * slot, slot, 2 * g + slot + 1)

            def w_hi(b, s):
                act.wait_ge(s_w, 4 * b + s + 1)
                act.activation(wT_hi[:, s % 2, :], w_f(s), ACT.Copy).then_inc(s_whi, 1)

            def v_block(b, first=0):
                for s in range(SLABS):
                    if s >= first:
                        split_hi(b + V0, s)
                    w_hi(b, s)
            v_block(0, first=2)
            with act.Fori(1, NB_V) as b:
                v_block(b)
            norm_scalar(act, 2)

        @block.vector
        def _(dv):
            done = [0]

            def link(ins):
                done[0] += 1
                ins.then_inc(s_dv, 1)
                dv.wait_ge(s_dv, done[0])

            def split_lo(B, s):
                dv.wait_ge(hi_ready, 4 * B + (s + 1))
                dv.tensor_tensor(lo[:, s % 2], raw[:, s, :].rearrange("p (c n) -> p c n", n=COLS),
                                 hi[:, s % 2].bitcast(f32), ALU.subtract).then_inc(lo_ready, 1)

            link(dv.memset(small[:, :], 0.0))
            dv.wait_ge(s_xhi, 1)
            dv.tensor_tensor(aT_lo[:, :, :], xs, aT_hi[:, :, :].bitcast(f32), ALU.subtract).then_inc(s_xlo, 1)
            dv.nop().then_inc(banks_free, 2)
            with dv.Fori(0, NB_IN) as b:
                for s in range(SLABS):
                    split_lo(b, s)

            dv.wait_ge(s_par, 48)
            link(dv.tensor_tensor(st[:, 192:320].rearrange("p (a d) -> p a d", d=QK_DIM),
                                  lamv[:, 0:4:2, :], lamv[:, 1:4:2, :], ALU.mult))
            dv.tensor_reduce(st[:, 128:130], st[:, 192:320].rearrange("p (a d) -> p a d", d=QK_DIM),
                             axis=AX.X, op=ALU.add).then_inc(s_lsum, 1)
            lam8, neg8 = par[:, 56:64], st[:, 0:8]
            link(dv.tensor_scalar(neg8, lam8, -1.0, None, ALU.mult))
            dv.tensor_tensor(neg8, neg8, lam8, ALU.min).then_inc(s_sp, 1)
            dv.wait_ge(s_u, 1)
            u8, r8, t8, q8 = st[:, 8:16], st[:, 80:88], st[:, 88:96], st[:, 96:104]
            link(dv.tensor_scalar(t8, u8, 2.0, None, ALU.add))
            link(dv.reciprocal(t8, t8))
            link(dv.tensor_tensor(r8, u8, t8, ALU.mult))
            link(dv.tensor_tensor(t8, r8, r8, ALU.mult))
            link(dv.memset(q8, 1.0 / 19))
            for n in range(8, -1, -1):
                link(dv.tensor_tensor(q8, q8, t8, ALU.mult))
                link(dv.tensor_scalar(q8, q8, 1.0 / (2 * n + 1), None, ALU.add))
            link(dv.tensor_tensor(q8, q8, r8, ALU.mult))
            link(dv.tensor_scalar(t8, lam8, -1.0, 0.0, ALU.mult, ALU.max))
            link(dv.scalar_tensor_tensor(q8, q8, 2.0, t8, ALU.mult, ALU.add))
            dv.tensor_scalar(st[:, 16:24], q8, 4.0, None, ALU.mult).then_inc(s_sp, 1)
            dv.wait_ge(s_lexp, 1)
            link(dv.tensor_tensor(st[:, 132:133], st[:, 131:132], st[:, 130:131], ALU.subtract))
            link(dv.tensor_scalar(st[:, 133:134], st[:, 132:133], -LAMBDA_INIT, None, ALU.add))

            for n in range(16):
                if n % 2 == 1:
                    dv.wait_ge(s_tr, n + 1)
                    dv.tensor_copy(front_target(n), ps4(4 + n % 4)).then_inc(s_trc[1], 1)
            link(dv.memset(xrT[:, :, 0:PAD], 0.0))
            dv.wait_ge(s_trc[0], 8)
            dv.wait_ge(s_trc[1], 8)
            for c in range(LRU_CHUNKS):
                link(dv.tensor_scalar(xc[:, c, :], xrT[:, c, 0:SEQ], conv_w(0, c), conv_b(c), ALU.mult, ALU.add))
                for j in (1, 2):
                    link(dv.scalar_tensor_tensor(xc[:, c, :], xrT[:, c, j:j + SEQ], conv_w(j, c), xc[:, c, :],
                                                 ALU.mult, ALU.add))
                dv.scalar_tensor_tensor(xc[:, c, :], xrT[:, c, 3:3 + SEQ], conv_w(3, c), xc[:, c, :],
                                        ALU.mult, ALU.add).then_inc(s_cp, 1)

            dv.wait_ge(s_cp, LRU_CHUNKS)
            dv.wait_ge(s_tanh, LRU_CHUNKS)
            dv.tensor_scalar(sq, th, 2.0 ** -116, None, ALU.max).then_inc(s_t2, 1)
            link(dv.tensor_scalar(rc, th, 1.0, None, ALU.add))
            link(dv.reciprocal(rc, rc))
            link(dv.tensor_scalar(th, th, -1.0, 1.0, ALU.mult, ALU.add))
            link(dv.tensor_tensor(th, th, rc, ALU.mult))
            link(dv.tensor_tensor(ig, ig, xc, ALU.mult))
            dv.wait_ge(s_sq, 1)
            link(dv.scalar_tensor_tensor(rc, sq, 2.0, rc, ALU.mult, ALU.mult))
            link(dv.tensor_tensor(ig, ig, rc, ALU.mult))
            for c in range(LRU_CHUNKS):
                last = dv.tensor_tensor_scan(rc[:, c, :], th[:, c, :], ig[:, c, :], 0.0, ALU.mult, ALU.add)
            link(last)
            dv.wait_ge(s_gx, 1)
            dv.tensor_tensor(xc, rc, xgT, ALU.mult).then_inc(s_lru, 1)

            def biased(h):
                dv.wait_ge(s_sc, h + 1)
                slope = 8.0 * 2.0 ** -(h + 1)
                link(dv.scalar_tensor_tensor(sx[:, h % 2], dist.unsqueeze(1).to_broadcast([P, 2, 384]), slope,
                                             ps[:, 4 + 2 * (h % 2):6 + 2 * (h % 2), 0:384], ALU.mult, ALU.add))
                mx = st[:, 32 + 4 * (h % 2):36 + 4 * (h % 2)].rearrange("p (c i) -> p c i", i=2)
                dv.tensor_reduce(mx[:, :, 0], sx[:, h % 2, :, 0:128], axis=AX.X, op=ALU.max)
                link(dv.tensor_reduce(mx[:, :, 1], sx[:, h % 2, :, 128:384], axis=AX.X, op=ALU.max))
                dv.tensor_scalar(st[:, 32 + 4 * (h % 2):36 + 4 * (h % 2)], st[:, 32 + 4 * (h % 2):36 + 4 * (h % 2)],
                                 -0.125, None, ALU.mult).then_inc(s_sx, 1)

            def mixed(h):
                dv.wait_ge(s_e, 4 * h + 4)
                sm = st[:, 40 + 4 * (h % 2):44 + 4 * (h % 2)]
                link(dv.reciprocal(sm, sm))
                link(dv.tensor_scalar(sm[:, 2:4], sm[:, 2:4], st[:, 133:134], None, ALU.mult))
                for i, keys in ((0, slice(0, 128)), (1, slice(128, 384))):
                    last = dv.tensor_scalar(sx[:, h % 2, 1, keys], sx[:, h % 2, 1, keys], sm[:, 2 + i:3 + i], None, ALU.mult)
                link(last)
                for i, keys in ((0, slice(0, 128)), (1, slice(128, 384))):
                    dv.scalar_tensor_tensor(sx[:, h % 2, 0, keys], sx[:, h % 2, 0, keys], sm[:, i:i + 1],
                                            sx[:, h % 2, 1, keys], ALU.mult, ALU.add).then_inc(s_pd, 1)

            for h in range(HEADS + 1):
                if h < HEADS:
                    if h >= 2:
                        dv.wait_ge(s_pt, h - 1)
                    biased(h)
                if h >= 1:
                    mixed(h - 1)
            dv.wait_ge(s_oc, HEADS)
            flat = at(20480, TILES * HEADS, P)
            ssq = at(4096, TILES * HEADS, P)
            link(dv.tensor_tensor(ssq, flat, flat, ALU.mult))
            link(dv.tensor_reduce(st[:, 48:64], ssq, axis=AX.X, op=ALU.add))
            dv.tensor_scalar(st[:, 48:64], st[:, 48:64], 1.0 / P, EPS, ALU.mult, ALU.add).then_inc(s_ms, 1)
            dv.wait_ge(s_rt, 1)
            newton(dv, link, st[:, 64:80], st[:, 48:64], st[:, 104:120])
            link(dv.tensor_scalar(st[:, 64:80], st[:, 64:80], 1.0 - LAMBDA_INIT, None, ALU.mult))
            link(dv.tensor_tensor(flat, flat, st[:, 64:80].unsqueeze(2).to_broadcast([P, 16, P]), ALU.mult))
            dv.tensor_tensor(flat, flat, subg.unsqueeze(1).to_broadcast([P, 16, P]), ALU.mult).then_inc(s_attn, 1)

            dv.wait_ge(s_lruhi, 1)
            dv.tensor_tensor(aT_lo[:, 8:16, :], xc, aT_hi[:, 8:16, :].bitcast(f32), ALU.subtract).then_inc(s_mlo, 1)

            def lo_from_psum(n, k, bank):
                dv.wait_ge(s_mhi, n + 1)
                dv.tensor_tensor(aT_lo[:, 2 * k:2 * k + 2, :], ps4(bank), aT_hi[:, 2 * k:2 * k + 2, :].bitcast(f32),
                                 ALU.subtract).then_inc(s_mlo, 1)
            for n in range(4):
                lo_from_psum(n, n, 4 + n)

            def take_mix(b):
                dv.wait_ge(slab_used, 4 * (OUT0 + 1) + 4 * b)
                dv.scalar_tensor_tensor(z_cols(4096, b), z_cols(14336, b), ALPHA, ps[:, bass.ds((b % 2) * 2, 2), :],
                                        ALU.mult, ALU.add).then_inc(banks_free, 1)

            def z_cols(off, b):
                return at(off, TILES, D_MODEL)[:, :, bass.ds(b * COLS, COLS)]

            for s in range(SLABS):
                split_lo(OUT0, s)
            dv.wait_ge(s_xn, 16)
            with dv.Fori(1, NB_OUT) as b:
                split_lo(b + OUT0, 0)
                split_lo(b + OUT0, 1)
                take_mix(b - 1)
                split_lo(b + OUT0, 2)
                split_lo(b + OUT0, 3)
            take_mix(NB_OUT - 1)
            dv.wait_ge(banks_free, 2 + NB_IN + NB_OUT)

            dv.wait_ge(s_ln1w, 32)
            norm_vector(dv, link, 0, lng, lnb, s_h)
            split_lo(WQ0, 0)
            for n in range(8):
                lo_from_psum(4 + n, n, 4 + n % 4)
            for s in range(1, SLABS):
                split_lo(WQ0, s)
            with dv.Fori(1, NB_WQ) as b:
                for s in range(SLABS):
                    split_lo(b + WQ0, s)
            for n in range(8):
                if n % 2 == 1:
                    dv.wait_ge(s_qt, n + 1)
                    dv.tensor_copy(pqT[:, 2 * n:2 * n + 2, :], ps4(4 + n % 4)).then_inc(s_qtc[1], 1)
            for n in range(8):
                if n % 2 == 1:
                    dv.wait_ge(s_scp, n + 1)
                    dv.tensor_copy(sc_bank(n), ps[:, n % 4, :]).then_inc(s_scc[1], 1)
            for taken in s_scc:
                dv.wait_ge(taken, 4)
            dv.nop().then_inc(s_htc, 1)

            dv.wait_ge(s_iota, 1)
            ROUTE_STEPS = 28

            def route(u):
                n = [0]

                def step(ins):
                    n[0] += 1
                    ins.then_inc(s_route, 1)
                    dv.wait_ge(s_route, ROUTE_STEPS * u + n[0])
                    dv.sem_inc(s_pass, 1)
                step(dv.tensor_copy(scu, sc_flat[:, bass.ds(u * (2 * P), 2 * P)].rearrange("p (a b) -> p a b", b=P)))
                for half in range(2):
                    first8, next8 = m32[:, half, 0:8], m32[:, half, 8:16]
                    step(dv.max(first8, scu[:, half, :]))
                    step(dv.max_index(ix[:, half, 0:8], first8, scu[:, half, :]))
                    step(dv.match_replace(rep[:, half, :], first8, scu[:, half, :], LOWEST))
                    step(dv.max(next8, rep[:, half, :]))
                    step(dv.max_index(ix[:, half, 8:16], next8, rep[:, half, :]))
                step(dv.tensor_copy(ixf, ix))
                step(dv.tensor_tensor(cand.rearrange("p (a b) -> p a b", b=TOPK),
                                      m32[:, 0, :].unsqueeze(2).to_broadcast([P, TOPK, TOPK]),
                                      m32[:, 1, :].unsqueeze(1).to_broadcast([P, TOPK, TOPK]), ALU.add))
                step(dv.max(top[:, 0:8], cand))
                step(dv.max_index(topix[:, 0:8], top[:, 0:8], cand))
                step(dv.match_replace(crep, top[:, 0:8], cand, LOWEST))
                step(dv.max(top[:, 8:16], crep))
                step(dv.max_index(topix[:, 8:16], top[:, 8:16], crep))
                step(dv.tensor_scalar(ab[:, 0, :], topix, 4, None, ALU.logical_shift_right))
                step(dv.tensor_scalar(ab[:, 1, :], topix, 15, None, ALU.bitwise_and))
                step(dv.tensor_copy(abf, ab))
                for half, keys in ((0, 20736), (1, 20992)):
                    step(dv.tensor_tensor(cmp[:, half], abf[:, half, :].unsqueeze(2).to_broadcast([P, TOPK, TOPK]),
                                          iota[:, 0:TOPK].unsqueeze(1).to_broadcast([P, TOPK, TOPK]), ALU.is_equal))
                    step(dv.tensor_tensor(cmp[:, half], cmp[:, half],
                                          ixf[:, half, :].unsqueeze(1).to_broadcast([P, TOPK, TOPK]), ALU.mult))
                    step(dv.tensor_reduce(arena[:, bass.ds(keys + u * TOPK, TOPK)], cmp[:, half],
                                          axis=AX.X, op=ALU.add))
                step(dv.tensor_copy(arena[:, bass.ds(20480 + u * TOPK, TOPK)], top))
                assert n[0] == ROUTE_STEPS, n[0]

            def take_gelu(j):
                dv.wait_ge(s_ht, j + 1)
                dv.tensor_copy(hT, ps[:, 4:6, :].rearrange("p a (c t) -> p (a c) t", t=SEQ)).then_inc(s_htc, 1)

            for s in range(SLABS):
                split_lo(U0, s)
            route(0)
            split_lo(U0 + 1, 0)
            split_lo(U0 + 1, 1)
            take_gelu(0)
            split_lo(U0 + 1, 2)
            split_lo(U0 + 1, 3)
            route(1)
            with dv.Fori(2, ROUTE) as j:
                split_lo(j + U0, 0)
                split_lo(j + U0, 1)
                dv.wait_ge(s_hts, 16 * j - 16)
                take_gelu(j - 1)
                split_lo(j + U0, 2)
                split_lo(j + U0, 3)
                route(j)
            link(dv.tensor_tensor(logits, gate_exp, gate_exp[:, :, 0:1].to_broadcast([P, ROUTE, TOPK]), ALU.subtract))
            dv.tensor_copy(gate_exp, logits).then_inc(s_gm, 1)
            with dv.Fori(ROUTE, NB_U) as j:
                split_lo(j + U0, 0)
                split_lo(j + U0, 1)
                dv.wait_ge(s_hts, 16 * j - 16)
                take_gelu(j - 1)
                split_lo(j + U0, 2)
                split_lo(j + U0, 3)
            dv.wait_ge(s_ge, 1)
            link(dv.tensor_reduce(gsum, gate_exp, axis=AX.X, op=ALU.add))
            link(dv.reciprocal(gsum, gsum))
            dv.tensor_tensor(gate_exp, gate_exp, gsum.unsqueeze(2).to_broadcast([P, ROUTE, TOPK]),
                             ALU.mult).then_inc(s_gt, 1)
            dv.wait_ge(s_hts, 16 * (NB_U - 1))
            take_gelu(NB_U - 1)
            dv.wait_ge(s_pk, 1)
            for i in range(TILES):
                dv.tensor_copy(picks[:, :, P * i:P * (i + 1)],
                               ps[:, 6 + i, 0:384].rearrange("p (w t) -> p w t", w=3)).then_inc(s_pkc, 1)
            dv.wait_ge(s_pkc, TILES)
            for s in range(2):
                split_lo(V0, s)

            def onehots(t0, slot):
                def col(w, t):
                    return picks[:, w, bass.ds(t0 + t, 1)]
                for t in range(4):
                    dv.tensor_scalar(onehot[:, slot, 0, t, :], iota[:, :], col(0, t), None, ALU.is_equal)
                    last = dv.tensor_scalar(onehot[:, slot, 1, t, :], iota[:, :], col(1, t), col(2, t),
                                            ALU.is_equal, ALU.mult)
                last.then_inc(s_oh, 1)
            dv.wait_ge(s_hts, 16 * NB_U)
            onehots(0, 0)
            onehots(4, 1)
            with dv.Fori(1, SEQ // 8) as g:
                for slot in range(2):
                    dv.wait_ge(s_G, 2 * g + (slot - 1))
                    onehots(8 * g + 4 * slot, slot)

            def product(b, s):
                n = 4 * b + s
                dv.wait_ge(s_hin[s // 2], 16 * b + 16)
                if not (isinstance(b, int) and n < 2):
                    dv.wait_ge(s_wlo, n - 1)
                dv.tensor_tensor(w_f(s), gates[:, bass.ds(n, 1), :].rearrange("p a t -> p (a t)"), hT[:, s, :],
                                 ALU.mult).then_inc(s_w, 1)

            def w_lo(b, s):
                dv.wait_ge(s_whi, 4 * b + s + 1)
                dv.tensor_tensor(wT_lo[:, s % 2, :], w_f(s), wT_hi[:, s % 2, :].bitcast(f32),
                                 ALU.subtract).then_inc(s_wlo, 1)

            def v_block(b, first=0, last=False):
                for s in range(SLABS):
                    if s < 3:
                        product(b, s + 1)
                    elif not last:
                        product(b + 1, 0)
                    if s >= first:
                        split_lo(b + V0, s)
                    w_lo(b, s)

            dv.wait_ge(s_Gc, SEQ // 4)
            product(0, 0)
            v_block(0, first=2)
            with dv.Fori(1, NB_V - 1) as b:
                v_block(b)
            v_block(NB_V - 1, last=True)

            dv.wait_ge(s_hre, 16)
            dv.wait_ge(slab_used, 4 * (V0 + NB_V))
            for i in range(TILES):
                link(dv.scalar_tensor_tensor(gates_z(i).rearrange("p (a n) -> p a n", n=COLS),
                                             h_back[:, i, :].rearrange("p (a n) -> p a n", n=COLS), ALPHA,
                                             ps[:, 4 * i:4 * i + 4, :], ALU.mult, ALU.add))
            dv.wait_ge(s_ln2w, 32)
            norm_vector(dv, link, 2, lng2, lnb2, s_y)

        @block.tensor
        def _(pe):
            def block_products(B, par_, hook=None):
                pe.wait_ge(banks_free, B + 1)
                for s in range(SLABS):
                    for part in range(2):
                        pe.wait_ge((hi_ready, lo_ready)[part], 4 * B + (s + 1))
                        for c in range(4):
                            k = 4 * s + c
                            for i in range(TILES):
                                o = ps[:, bass.ds(par_ * 2 + i, 1), :].rearrange("p a n -> p (a n)")
                                t = slice(P * i, P * (i + 1))
                                if part == 0:
                                    pe.matmul(o, aT_hi[:, k, t], hi[:, s % 2, c], start=(k == 0), stop=False)
                                    pe.matmul(o, aT_lo[:, k, t], hi[:, s % 2, c], start=False, stop=False)
                                else:
                                    last = pe.matmul(o, aT_hi[:, k, t], lo[:, s % 2, c], start=False, stop=(k == 15))
                    last.then_inc(slab_used, 1)
                    if s == 0 and hook:
                        hook()

            pe.wait_ge(s_xlo, 1)
            with pe.Fori(0, NB_IN) as b:
                block_products(b, b % 2)

            pe.wait_ge(s_const, 6)
            pe.wait_ge(banks_free, NB_IN + 2)
            for n in range(16):
                if n >= 4:
                    pe.wait_ge(s_trc[n % 2], (n - 4) // 2 + 1)
                kind, c0 = n // 4, 2 * (n % 4)
                first_block = (4, 6, 0, 2)[kind]
                for c in (c0, c0 + 1):
                    for i in range(TILES):
                        src = proj[:, first_block + c // 4, i, (c % 4) * P:(c % 4 + 1) * P]
                        last = pe.transpose(ps[:, 4 + n % 4, (2 * (c - c0) + i) * P:(2 * (c - c0) + i + 1) * P],
                                            src, ident)
                last.then_inc(s_tr, 1)

            for taken in s_trc:
                pe.wait_ge(taken, 8)
            for c in range(LRU_CHUNKS):
                pe.wait_ge(s_cp, c + 1)
                if c >= 4:
                    pe.wait_ge(s_sig, 2 * (c - 3))
                if c == 0:
                    pe.wait_ge(s_rg, 16)
                pe.matmul(ps[:, 4 + c % 4, 0:SEQ], rg_a(c), xc[:, c, :], start=True, stop=True)
                pe.matmul(ps[:, 4 + c % 4, SEQ:2 * SEQ], rg_x(c), xc[:, c, :], start=True, stop=True)\
                    .then_inc(s_gate, 1)

            def scores(h):
                if h < 2:
                    pe.wait_ge(s_sig, 16)
                else:
                    pe.wait_ge(s_sx, h - 1)
                for c in range(2):
                    rows = slice(QK_DIM * c, QK_DIM * (c + 1))
                    bank = 4 + 2 * (h % 2) + c
                    pe.matmul(ps[:, bank, 0:128], qT[rows, h, 0:128], kT[rows, h, 0:128], start=True, stop=True)
                    last = pe.matmul(ps[:, bank, 128:384], qT[rows, h, 128:256], kT[rows, h, :], start=True, stop=True)
                last.then_inc(s_sc, 1)

            def values(h):
                pe.wait_ge(s_pd, 2 * h + 2)
                if h >= 2:
                    pe.wait_ge(s_ptc, h - 1)
                for n, keys in enumerate((slice(0, 128), slice(128, 256), slice(256, 384))):
                    last = pe.transpose(ps[:, h % 2, P * n:P * (n + 1)], sx[:, h % 2, 0, keys], ident)
                last.then_inc(s_pt, 1)
                pe.wait_ge(s_ptc, h + 1)
                if h >= 2:
                    pe.wait_ge(s_oc, h - 1)

                def v_of(tile):
                    return proj[:, 8 + h // 4, tile, (h % 4) * P:(h % 4 + 1) * P]
                o = ps[:, 2 + h % 2, :]
                pe.matmul(o[:, 0:P], pdT[:, h % 2, 0, :], v_of(0), start=True, stop=True)
                pe.matmul(o[:, P:2 * P], pdT[:, h % 2, 1, :], v_of(0), start=True, stop=False)
                pe.matmul(o[:, P:2 * P], pdT[:, h % 2, 2, :], v_of(1), start=False, stop=True).then_inc(s_o, 1)

            for h in range(HEADS + 1):
                if h < HEADS:
                    scores(h)
                if h >= 1:
                    values(h - 1)

            pe.wait_ge(s_attn, 1)
            for n in range(4):
                for c in (2 * n, 2 * n + 1):
                    for i in range(TILES):
                        last = pe.transpose(ps[:, 4 + n, (2 * (c % 2) + i) * P:(2 * (c % 2) + i + 1) * P],
                                            att[:, i, c, :], ident)
                last.then_inc(s_mt, 1)

            pe.wait_ge(s_mlo, 5)
            with pe.Fori(0, NB_OUT) as b:
                block_products(b + OUT0, b % 2)

            pe.wait_ge(s_h, 2)
            for n in range(8):
                if n >= 4:
                    pe.wait_ge(s_mlo, 5 + n - 3)
                for c in (2 * n, 2 * n + 1):
                    for i in range(TILES):
                        last = pe.transpose(ps[:, 4 + n % 4, (2 * (c % 2) + i) * P:(2 * (c % 2) + i + 1) * P],
                                            z[:, i, P * c:P * (c + 1)], ident)
                last.then_inc(s_mt, 1)
            pe.wait_ge(s_mlo, 13)
            with pe.Fori(0, NB_WQ) as b:
                block_products(b + WQ0, b % 2)

            pe.wait_ge(banks_free, 2 + U0)
            for n in range(8):
                if n >= 4:
                    pe.wait_ge(s_qtc[n % 2], (n - 4) // 2 + 1)
                for c in (2 * n, 2 * n + 1):
                    for i in range(TILES):
                        last = pe.transpose(ps[:, 4 + n % 4, (2 * (c % 2) + i) * P:(2 * (c % 2) + i + 1) * P],
                                            pq[:, c // 4, i, (c % 4) * P:(c % 4 + 1) * P], ident)
                last.then_inc(s_qt, 1)
            for taken in s_qtc:
                pe.wait_ge(taken, 4)
            pe.wait_ge(s_sk, 16)
            for n in range(8):
                if n >= 4:
                    pe.wait_ge(s_scc[n % 2], (n - 4) // 2 + 1)
                i = n // 4
                for m in range(4):
                    hp = 4 * (n % 4) + m
                    last = pe.matmul(ps[:, n % 4, P * m:P * (m + 1)], pqT[:, hp, P * i:P * (i + 1)], skT[:, hp, :],
                                     start=True, stop=True)
                last.then_inc(s_scp, 1)
            for taken in s_scc:
                pe.wait_ge(taken, 4)

            def gelu_transposes(j):
                pe.wait_ge(banks_free, j + U0 + 3)
                pe.wait_ge(s_htc, j + 1)
                for c in range(4):
                    for i in range(TILES):
                        o = (2 * (c % 2) + i) * P
                        last = pe.transpose(ps[:, 4 + c // 2, o:o + P], gs[:, i, P * c:P * (c + 1)], ident)
                last.then_inc(s_ht, 1)

            block_products(U0, 0)
            with pe.Fori(1, NB_U) as j:
                block_products(j + U0, j % 2, hook=lambda: gelu_transposes(j - 1))
            gelu_transposes(NB_U - 1)

            pe.wait_ge(s_gt, 1)
            for i in range(TILES):
                for w, src in enumerate((20736, 20992, 20480)):
                    last = pe.transpose(ps[:, 6 + i, P * w:P * (w + 1)], at(src + i * P, P), ident)
            last.then_inc(s_pk, 1)
            def gate_products(slot):
                for t in range(4):
                    last = pe.matmul(ps[:, slot, P * t:P * (t + 1)], onehot[:, slot, 1, t, :],
                                     onehot[:, slot, 0, t, :], start=True, stop=True)
                last.then_inc(s_G, 1)
            for slot in range(2):
                pe.wait_ge(s_oh, slot + 1)
                gate_products(slot)
            with pe.Fori(1, SEQ // 8) as g:
                for slot in range(2):
                    pe.wait_ge(s_oh, 2 * g + (slot + 1))
                    pe.wait_ge(s_Gc, 2 * g + (slot - 1))
                    gate_products(slot)

            def v_block(b, first=False, last=False):
                for s in range(SLABS):
                    n = 4 * b + s
                    start, stop = first and s == 0, last and s == 3
                    for part, (w, v) in enumerate(((wT_hi, hi), (wT_lo, hi), (wT_hi, lo))):
                        if part == 0:
                            pe.wait_ge(s_whi, n + 1)
                            pe.wait_ge(hi_ready, n + (4 * V0 + 1))
                        elif part == 1:
                            pe.wait_ge(s_wlo, n + 1)
                        else:
                            pe.wait_ge(lo_ready, n + (4 * V0 + 1))
                        for i in range(TILES):
                            for c in range(4):
                                done = pe.matmul(ps[:, 4 * i + c, :], w[:, s % 2, P * i:P * (i + 1)], v[:, s % 2, c],
                                                 start=start and part == 0, stop=stop and part == 2)
                    done.then_inc(slab_used, 1)
            pe.wait_ge(s_Gc, SEQ // 4)
            v_block(0, first=True)
            with pe.Fori(1, NB_V - 1) as b:
                v_block(b)
            v_block(NB_V - 1, last=True)


def kernel(**inputs):
    import concourse.bacc as bacc
    from concourse.bass_utils import run_bass_kernel_spmd as run

    a = {k: np.asarray(v) for k, v in inputs.items()}

    def blocks(w):
        n = w.shape[1] // 512
        return np.ascontiguousarray(w.reshape(4, 4, 128, n, 512).transpose(3, 0, 2, 1, 4)).reshape(n, 4, 128, 2048)

    x = a["x"][0]
    w_in = a["w_in"][0]
    q, k, v, xr, xg = (w_in[:, 1024 * n:1024 * (n + 1)] for n in range(5))
    col = lambda t: t.reshape(-1, 8, 128).transpose(2, 0, 1).reshape(128, -1)
    arrays = {
        "xT": x.T.reshape(16, 128, 256).transpose(1, 0, 2),
        "x": x,
        "w_in": blocks(np.concatenate([xr, xg, q, k, v], axis=1)),
        "w_out": blocks(a["w_out"][0]),
        "w_q": blocks(a["peer_wq"][0]),
        "uT": blocks(a["peer_u"][0].T),
        "v_tab": a["peer_v"][0].reshape(32, 4, 128, 2048),
        "subkeysT": a["peer_subkeys"][0].reshape(16, 128, 128).transpose(2, 0, 1),
        "params": np.concatenate([col(a["conv_w"][0]), col(a["conv_b"]), col(a["b_rg_a"].reshape(1, 1024)),
                                  col(a["b_rg_x"].reshape(1, 1024)), col(a["lru_lambda"])], axis=1),
        "lambdas": np.concatenate([a["lambda_q1"], a["lambda_k1"], a["lambda_q2"], a["lambda_k2"]], axis=0),
        "subln_g": a["subln_g"][0],
        "ln1_g": a["ln1_g"][0], "ln1_b": a["ln1_b"][0], "ln2_g": a["ln2_g"][0], "ln2_b": a["ln2_b"][0],
        "w_rg": np.stack([a["w_rg_a"][0], a["w_rg_x"][0]]).transpose(2, 0, 1, 3),
    }
    arrays = {n: np.ascontiguousarray(t) for n, t in arrays.items()}
    nc = bacc.Bacc("TRN2", target_bir_lowering=False, num_devices=1)
    f32 = mybir.dt.float32
    args = {n: nc.dram_tensor(n + "_dram", t.shape, f32, kind="ExternalInput").ap() for n, t in arrays.items()}
    out = nc.dram_tensor("out_dram", (1, 256, 2048), f32, kind="ExternalOutput").ap()
    gelu_dram = nc.dram_tensor("gelu_dram", (32, 128, 4, 256), f32, kind="Internal").ap()
    h_dram = nc.dram_tensor("h_dram", (256, 2048), f32, kind="Internal").ap()
    hybrid_layer(nc, **args, out=out, gelu_dram=gelu_dram, h_dram=h_dram)
    r = run(nc, [{n + "_dram": t for n, t in arrays.items()}], core_ids=[0])
    return r.results[0]["out_dram"]
```

```python
import math

import numpy as np

import concourse.bass as bass
from concourse import mybir
from contextlib import ExitStack


def hybrid_layer(nc, xT, x, w_in, w_out, w_q, uT, v_tab, subkeysT, params, lambdas, subln_g, w_rg,
                 ln1_g, ln1_b, ln2_g, ln2_b, out, gelu_dram, h_dram):
    f32, f32r, u32 = mybir.dt.float32, mybir.dt.float32r, mybir.dt.uint32
    ALU, ACT, AX = mybir.AluOpType, mybir.ActivationFunctionType, mybir.AxisListType

    P = 128
    D_MODEL = 2048
    SEQ = 256
    TILES = SEQ // P
    KC = D_MODEL // P
    COLS = 512
    SLABS = 4
    HEADS = 8
    QK_DIM = 64
    TOPK = 16
    LRU_CHUNKS = 8
    PAD = 3
    XROW = SEQ + PAD
    ALPHA = 2.0 ** 0.25
    EPS = 1e-5
    LAMBDA_INIT = 0.8 - 0.6 * math.exp(0.0)
    MASKED = -1e30
    LOWEST = -3.0e38

    IN0, OUT0, WQ0, U0, V0 = 0, 10, 14, 18, 50
    NB_IN, NB_OUT, NB_WQ, NB_U, NB_V = 10, 4, 4, 32, 32
    ROUTE = TILES * HEADS

    ctx = ExitStack()
    with ctx:
        def sb(name, shape, dt=f32, stack=ctx):
            return stack.enter_context(nc.sbuf_tensor(name, shape, dt))

        def sem(name):
            return ctx.enter_context(nc.semaphore(name))

        raw = sb("raw", [P, SLABS, 2048])
        hi = sb("slab_hi", [P, 2, 4, COLS], f32r)
        lo = sb("slab_lo", [P, 2, 4, COLS], f32r)
        stage = sb("stage", [P, 2048])
        small = sb("small", [P, 768])
        picks_scope = ExitStack()
        picks = sb("picks", [P, 3, SEQ], stack=picks_scope)
        iota = sb("iota", [P, P], stack=picks_scope)
        picks_scope.close()
        wT_hi = sb("wT_hi", [P, 2, SEQ], f32r)
        wT_lo = sb("wT_lo", [P, 2, SEQ], f32r)
        front = ExitStack()
        aT_hi = sb("aT_hi", [P, KC, SEQ], f32r, front)
        aT_lo = sb("aT_lo", [P, KC, SEQ], f32r, front)
        arena = sb("arena", [P, 24576], f32, front)
        front.close()
        gflat = sb("gates", [P, P * SEQ])
        ps = ctx.enter_context(nc.psum_tensor("ps", [P, 8, COLS], f32))

        def at(off, *dims):
            n = int(np.prod(dims))
            v = arena[:, off:off + n]
            if len(dims) == 1:
                return v
            names = "abcd"[:len(dims)]
            return v.rearrange(f"p ({' '.join(names)}) -> p {' '.join(names)}",
                               **{k: d for k, d in zip(names, dims)})

        xs = at(0, KC, SEQ)
        proj = at(4096, NB_IN, TILES, COLS)
        qT, kT = at(14336, HEADS, SEQ), at(16384, HEADS, SEQ)
        xgT = at(18432, LRU_CHUNKS, SEQ)
        xrT = at(8192, LRU_CHUNKS, XROW)
        xc, th = at(0, LRU_CHUNKS, SEQ), at(2048, LRU_CHUNKS, SEQ)
        ig, rc = at(4096, LRU_CHUNKS, SEQ), at(6144, LRU_CHUNKS, SEQ)
        sq = at(8192, LRU_CHUNKS, SEQ)
        att = at(20480, TILES, HEADS, P)
        dist = at(22528, 384)
        sx = at(10272, 2, 2, 384)
        pdT = at(22912, 2, 3, P)
        par = at(23680, 64)
        lamv = at(23744, 4, QK_DIM)
        subg = at(24000, P)
        st = at(24128, 320)
        ident = small[:, 256:256 + P]
        xn = at(14336, TILES, D_MODEL)
        z = at(4096, TILES, D_MODEL)
        lng, lnb = at(8192, D_MODEL), at(10240, D_MODEL)
        pq = at(0, NB_WQ, TILES, COLS)
        pqT = at(8192, 2 * HEADS, SEQ)
        skT = at(12288, 2 * HEADS, P)
        sc = at(14336, TILES, 2 * HEADS * P)
        sc_flat = at(14336, TILES * 2 * HEADS * P)
        gs = at(0, TILES, COLS)

        conv_w = lambda j, c: par[:, 8 * j + c:8 * j + c + 1]
        conv_b = lambda c: par[:, 32 + c:33 + c]
        b_a = lambda c: par[:, 40 + c:41 + c]
        b_x = lambda c: par[:, 48 + c:49 + c]

        rg_a = lambda c: stage[:, P * c:P * (c + 1)]
        rg_x = lambda c: stage[:, 1024 + P * c:1024 + P * (c + 1)]
        hT = stage[:, 0:1024].rearrange("p (c t) -> p c t", t=SEQ)

        EARLY = 80
        LATE = SEQ - EARLY
        BATCHES, LATE_BATCHES = SEQ // 4, LATE // 4
        GATE_BLOCK = NB_U - LATE_BATCHES // SLABS
        gates_early = gflat[:, 0:P * EARLY].rearrange("p (i t) -> p i t", t=EARLY)
        gates_late = gflat[:, P * EARLY:].rearrange("p (i t) -> p i t", t=LATE)

        def hot(view):
            return view.rearrange("p (w t k) -> p w t k", w=2, t=4)
        hot_late = [hot(stage[:, 1024:2048]), hot(at(1024, 1024))]
        hot_early = [hot(stage[:, 1024:2048]), hot(raw[:, 2, 0:1024]), hot(raw[:, 2, 1024:2048]), hot(raw[:, 3, 0:1024])]

        LAST = P * EARLY
        h_back = gflat[:, LAST:LAST + 4096].rearrange("p (i d) -> p i d", d=D_MODEL)
        lng2, lnb2 = gflat[:, LAST + 4096:LAST + 6144], gflat[:, LAST + 6144:LAST + 8192]

        def gates_z(i):
            return gflat[:, LAST + 8192 + i * D_MODEL:LAST + 8192 + (i + 1) * D_MODEL]

        def ps4(bank):
            return ps[:, bank, :].rearrange("p (c t) -> p c t", t=SEQ)

        def front_target(n):
            kind, c = n // 4, 2 * (n % 4)
            if kind == 2:
                return xrT[:, c:c + 2, PAD:]
            return (qT, kT, None, xgT)[kind][:, c:c + 2, :]

        def sc_bank(n):
            return sc[:, n // 4, (n % 4) * 512:(n % 4 + 1) * 512]

        def w_f(s):
            return small[:, 256 + (s % 2) * SEQ:256 + (s % 2 + 1) * SEQ]

        FOUND = 21504
        match = at(1024, 8, TOPK, TOPK)
        places = at(3072, 2, ROUTE, TOPK).bitcast(u32)
        places_f = at(3584, 2, ROUTE, TOPK)
        keys_f = at(4096, ROUTE, 2, TOPK)
        scu = at(18432, 2, P)
        rep = at(18688, 2, P)
        cand, crep = at(18944, 256), at(19200, 256)
        found = at(19456, 64).bitcast(u32)
        top, topix = at(19456, TOPK), at(19472, TOPK).bitcast(u32)
        ix = at(19488, 2, TOPK).bitcast(u32)
        m32 = at(19520, 2, TOPK)
        all_found = at(FOUND, ROUTE, 64)
        top_all = all_found[:, :, 0:16]
        cand_ix = all_found[:, :, 16:32].bitcast(u32)
        key_ix = all_found[:, :, 32:64].rearrange("p u (a k) -> p u a k", a=2).bitcast(u32)
        gate_exp = at(20480, ROUTE, TOPK)
        key_a = at(20736, ROUTE, TOPK)
        key_b = at(20992, ROUTE, TOPK)
        gsum = at(21248, ROUTE)

        def stat(i, base, a, n=1):
            o = 128 * (base // 2) + 64 * i + a
            return small[:, o:o + n]

        def norm_scalar(act, base):
            for i in range(TILES):
                act.wait_ge(s_var, base + i + 1)
                act.activation(stat(i, base, 27), stat(i, base, 26), ACT.Sqrt).then_inc(s_std, 1)

        loaded = [sem(f"slab_loaded_{s}") for s in range(SLABS)]
        hi_ready, lo_ready, slab_used = sem("hi_ready"), sem("lo_ready"), sem("slab_used")
        banks_free = sem("banks_free")
        s_const, s_par, s_xs = sem("const_ready"), sem("params_loaded"), [sem(f"xT_loaded_{s}") for s in range(SLABS)]
        s_xhi, s_xlo = sem("x_hi_ready"), sem("x_lo_ready")
        s_tr = sem("front_transposed")
        s_trc, s_qtc, s_scc = ([sem(f"{n}_by_{e}") for e in ("act", "dve")]
                               for n in ("front_transposes_taken", "q_transposes_taken", "key_scores_taken"))
        s_cp = sem("conv_done")
        s_gate, s_sig = sem("lru_gates_in_psum"), sem("lru_sigmoid_done")
        s_tanh, s_sp, s_u, s_t2, s_sq = (sem("lru_tanh_done"), sem("lru_rate_ready"), sem("lru_exp_done"),
                                         sem("lru_tanh_clamped"), sem("lru_sqrt_done"))
        s_gx, s_lru, s_lruhi = sem("xg_gelu_done"), sem("lru_done"), sem("lru_hi_ready")
        s_lexp, s_lsum = sem("lambda_exp_done"), sem("lambda_sums_ready")
        s_sc, s_sx, s_e, s_pd = sem("scores_in_psum"), sem("scores_biased"), sem("exp_done"), sem("probs_ready")
        s_pt, s_ptc, s_o, s_oc = sem("probs_transposed"), sem("probs_transposes_taken"), sem("att_in_psum"), sem("att_taken")
        s_ms, s_rt, s_attn = sem("att_mean_square"), sem("att_root"), sem("att_normed")
        s_mt, s_mhi, s_mlo = sem("mix_transposed"), sem("mix_hi_ready"), sem("mix_lo_ready")
        s_xn, s_ln1w, s_z = sem("x_loaded"), sem("ln1_weights_loaded"), sem("residual_ready")
        s_var, s_std, s_nb, s_nrm = sem("variance_ready"), sem("std_ready"), sem("norm_bias_ready"), sem("normed")
        s_h, s_hst = sem("h_ready"), sem("h_stored")
        s_sk = sem("subkeys_loaded")
        s_qt, s_scp = sem("q_transposed"), sem("key_scores_in_psum")
        s_gelu, s_ht, s_htc, s_hts = sem("gelu_done"), sem("gelu_transposed"), sem("gelu_transposes_taken"), sem("gelu_stored")
        s_route, s_pass = sem("route_chain"), sem("route_passed")
        s_gm, s_ge, s_gt = sem("gate_logits_ready"), sem("gate_exp_done"), sem("gates_ready")
        s_pk, s_pkc = sem("picks_transposed"), sem("picks_ready")
        s_iota, s_rg = sem("iota_ready"), sem("lru_gate_weights_loaded")
        s_oh0, s_oh, s_G, s_Gc = sem("onehots_ready"), sem("onehots_weighed"), sem("gates_in_psum"), sem("gates_taken")
        s_hin = [sem("gelu_loaded_0"), sem("gelu_loaded_1")]
        s_w, s_whi, s_wlo = sem("w_ready"), sem("w_hi_ready"), sem("w_lo_ready")
        s_hre, s_ln2w, s_z2 = sem("h_reloaded"), sem("ln2_weights_loaded"), sem("residual2_ready")
        s_y, s_out = sem("y_ready"), sem("out_stored")
        s_dv = sem("vector_chain")

        block = ctx.enter_context(nc.Block())

        def newton(dv, link, root, var, tmp):
            link(dv.reciprocal(root, root))
            link(dv.tensor_tensor(tmp, root, root, ALU.mult))
            link(dv.tensor_tensor(tmp, tmp, var, ALU.mult))
            link(dv.tensor_scalar(tmp, tmp, -0.5, 1.5, ALU.mult, ALU.add))
            link(dv.tensor_tensor(root, root, tmp, ALU.mult))

        def norm_stats(dv, link, base, i, zt):
            for k in range(4):
                last = dv.bn_stats(stat(i, base, 6 * k, 6), zt[:, COLS * k:COLS * (k + 1)])
            link(last)
            link(dv.bn_aggr(stat(i, base, 24, 2), stat(i, base, 0, 24)))
            dv.tensor_scalar(stat(i, base, 26), stat(i, base, 25), EPS, None, ALU.add).then_inc(s_var, 1)

        def norm_apply(dv, link, base, i, zt, g, b, ready, pieces=1):
            dv.wait_ge(s_std, base + i + 1)
            newton(dv, link, stat(i, base, 27), stat(i, base, 26), stat(i, base, 28))
            link(dv.scalar_tensor_tensor(zt, zt, stat(i, base, 24), g, ALU.subtract, ALU.mult))
            n = D_MODEL // pieces
            for k in range(0, D_MODEL, n):
                dv.scalar_tensor_tensor(zt[:, k:k + n], zt[:, k:k + n], stat(i, base, 27), b[:, k:k + n],
                                        ALU.mult, ALU.add).then_inc(ready, 1)

        @block.sync
        def _(sp):
            def stream(src, blocks, base, first=0):
                with sp.Fori(first, blocks) as b:
                    for s in range(SLABS):
                        sp.wait_ge(lo_ready, 4 * b + (4 * base + s - 3))
                        sp.dma_start(raw[:, s, :], src[b, s]).then_inc(loaded[s], 16)

            for s in range(SLABS):
                sp.dma_start(xs[:, 4 * s:4 * s + 4, :], xT[:, 4 * s:4 * s + 4, :]).then_inc(s_xs[s], 16)
                sp.dma_start(raw[:, s, :], w_in[0, s]).then_inc(loaded[s], 16)
            stream(w_in, NB_IN, IN0, first=1)
            stream(w_out, NB_OUT, OUT0)
            stream(w_q, NB_WQ, WQ0)
            stream(uT, NB_U, U0)
            for s in range(SLABS):
                if s >= 2:
                    sp.wait_ge(s_G, BATCHES)
                sp.wait_ge(lo_ready, 4 * V0 + s - 3)
                sp.dma_start(raw[:, s, :], v_tab[0, s]).then_inc(loaded[s], 16)
            stream(v_tab, NB_V, V0, first=1)
            out_v = out.rearrange("b (i p) d -> p (b i) d", p=P)
            for n in range(2 * TILES):
                i, cols = n // 2, slice(1024 * (n % 2), 1024 * (n % 2) + 1024)
                sp.wait_ge(s_y, n + 1)
                sp.dma_start(out_v[:, i, cols], gates_z(i)[:, cols]).then_inc(s_out, 16)
            sp.wait_ge(s_out, 16 * 2 * TILES)

        @block.gpsimd
        def _(pool):
            pool.memset(ident, 0.0).then_inc(s_const, 1)
            pool.dma_start(stage[:, :].rearrange("p (w h j) -> p w h j", w=2, h=LRU_CHUNKS), w_rg).then_inc(s_rg, 16)
            pool.iota(dist[:, 0:128], [[1, 128]], base=0, channel_multiplier=-1,
                      allow_small_or_imprecise_dtypes=True).then_inc(s_const, 1)
            pool.iota(dist[:, 128:384], [[1, 256]], base=-P, channel_multiplier=-1,
                      allow_small_or_imprecise_dtypes=True).then_inc(s_const, 1)
            pool.iota(iota[:, :], [[1, P]], base=0, channel_multiplier=0,
                      allow_small_or_imprecise_dtypes=True).then_inc(s_iota, 1)
            pool.wait_ge(s_const, 3)
            pool.affine_select(out=ident, in_=ident, compare_op=ALU.not_equal, fill=1.0, base=0,
                               pattern=[[-1, P]], channel_multiplier=1).then_inc(s_const, 1)
            pool.affine_select(out=dist[:, 0:128], in_=dist[:, 0:128], compare_op=ALU.is_ge, fill=MASKED,
                               base=0, pattern=[[-1, 128]], channel_multiplier=1).then_inc(s_const, 1)
            pool.affine_select(out=dist[:, 128:384], in_=dist[:, 128:384], compare_op=ALU.is_ge, fill=MASKED,
                               base=P, pattern=[[-1, 256]], channel_multiplier=1).then_inc(s_const, 1)
            pool.dma_start(par, params).then_inc(s_par, 16)
            pool.dma_start(lamv, lambdas.partition_broadcast(P)).then_inc(s_par, 16)
            pool.dma_start(subg, subln_g.partition_broadcast(P)).then_inc(s_par, 16)
            pool.wait_ge(s_attn, 1)
            pool.dma_start(xn, x.rearrange("(i p) d -> p i d", p=P)).then_inc(s_xn, 16)
            pool.wait_ge(s_lru, 1)
            pool.dma_start(lng, ln1_g.partition_broadcast(P)).then_inc(s_ln1w, 16)
            pool.dma_start(lnb, ln1_b.partition_broadcast(P)).then_inc(s_ln1w, 16)
            pool.dma_start(skT, subkeysT).then_inc(s_sk, 16)
            pool.wait_ge(s_h, 2)
            pool.dma_start(h_dram.rearrange("(i p) d -> p i d", p=P), z).then_inc(s_hst, 16)
            pool.wait_ge(s_hst, 16)
            pool.wait_ge(s_htc, 2)
            pool.dma_start(gelu_dram[0], hT).then_inc(s_hts, 16)
            def store_gelu(j):
                pool.wait_ge(s_htc, j + 2)
                pool.dma_start(gelu_dram[j], hT).then_inc(s_hts, 16)

            def weigh(m, t0, view):
                pool.wait_ge(s_oh0, m + 1)
                pool.tensor_tensor(view[:, 1], view[:, 1],
                                   picks[:, 2, bass.ds(t0, 4)].unsqueeze(2).to_broadcast([P, 4, P]), ALU.mult)\
                    .then_inc(s_oh, 1)

            with pool.Fori(1, GATE_BLOCK - 1) as j:
                store_gelu(j)
            with pool.Fori(GATE_BLOCK, NB_U) as j:
                for s in range(SLABS):
                    m = SLABS * j + (s - SLABS * GATE_BLOCK)
                    weigh(m, 4 * m + EARLY, hot_late[s % 2])
                    if s == 0:
                        store_gelu(j - 1)
            for k in range(4):
                weigh(LATE_BATCHES + k, 4 * k, hot_early[k])
            store_gelu(NB_U - 1)
            with pool.Fori(1, (BATCHES - LATE_BATCHES) // 4) as g:
                for k in range(4):
                    weigh(4 * g + (LATE_BATCHES + k), 16 * g + 4 * k, hot_early[k])
            pool.wait_ge(s_hts, 16 * NB_U)
            for half in range(2):
                pool.dma_start(hT[:, 2 * half:2 * half + 2, :], gelu_dram[0, :, 2 * half:2 * half + 2, :])\
                    .then_inc(s_hin[half], 16)
            with pool.Fori(1, NB_V) as b:
                for half in range(2):
                    pool.wait_ge(s_w, 4 * b + (2 * half - 2))
                    pool.dma_start(hT[:, 2 * half:2 * half + 2, :], gelu_dram[b, :, 2 * half:2 * half + 2, :])\
                        .then_inc(s_hin[half], 16)
            pool.dma_start(h_back, h_dram.rearrange("(i p) d -> p i d", p=P)).then_inc(s_hre, 16)
            pool.dma_start(lng2, ln2_g.partition_broadcast(P)).then_inc(s_ln2w, 16)
            pool.dma_start(lnb2, ln2_b.partition_broadcast(P)).then_inc(s_ln2w, 16)

        @block.scalar
        def _(act):
            def split_hi(B, s, reused=True):
                act.wait_ge(loaded[s], 16 * B + 16)
                if reused:
                    act.wait_ge(slab_used, 4 * B + (s - 1))
                act.activation(hi[:, s % 2], raw[:, s, :].rearrange("p (c n) -> p c n", n=COLS),
                               ACT.Copy).then_inc(hi_ready, 1)

            def pair(par_):
                return ps[:, bass.ds(par_ * 2, 2), :]

            for s in range(SLABS):
                piece = slice(4 * s, 4 * s + 4)
                act.wait_ge(s_xs[s], 16)
                act.activation(aT_hi[:, piece, :], xs[:, piece, :], ACT.Copy).then_inc(s_xhi, 1)
                split_hi(IN0, s, reused=s >= 2)

            def take_proj(b):
                act.wait_ge(slab_used, 4 * b + 4)
                act.activation(proj_block(b), pair(b % 2), ACT.Copy).then_inc(banks_free, 1)

            def proj_block(b):
                return arena[:, bass.ds(4096 + b * (TILES * COLS), TILES * COLS)]\
                    .rearrange("p (i n) -> p i n", n=COLS)

            with act.Fori(1, NB_IN) as b:
                split_hi(b, 0)
                split_hi(b, 1)
                take_proj(b - 1)
                split_hi(b, 2)
                split_hi(b, 3)
            take_proj(NB_IN - 1)

            act.wait_ge(s_sp, 1)
            act.activation(st[:, 8:16], st[:, 0:8], ACT.Exp).then_inc(s_u, 1)
            act.wait_ge(s_lsum, 1)
            act.activation(st[:, 130:132], st[:, 128:130], ACT.Exp).then_inc(s_lexp, 1)
            for n in range(16):
                if n % 2 == 0:
                    act.wait_ge(s_tr, n + 1)
                    act.activation(front_target(n), ps4(4 + n % 4), ACT.Copy).then_inc(s_trc[0], 1)

            for c in range(LRU_CHUNKS):
                act.wait_ge(s_gate, c + 1)
                act.activation(th[:, c, :], ps[:, 4 + c % 4, 0:SEQ], ACT.Sigmoid, bias=b_a(c)).then_inc(s_sig, 1)
                act.activation(ig[:, c, :], ps[:, 4 + c % 4, SEQ:2 * SEQ], ACT.Sigmoid, bias=b_x(c)).then_inc(s_sig, 1)
            act.wait_ge(s_sig, 16)
            act.wait_ge(s_sp, 2)
            for c in range(LRU_CHUNKS):
                act.activation(th[:, c, :], th[:, c, :], ACT.Tanh, scale=st[:, 16 + c:17 + c]).then_inc(s_tanh, 1)
            act.wait_ge(s_trc[1], 8)
            act.wait_ge(s_trc[0], 8)
            act.activation(xgT, xgT, ACT.Gelu_apprx_tanh).then_inc(s_gx, 1)
            act.wait_ge(s_t2, 1)
            act.activation(sq, sq, ACT.Sqrt).then_inc(s_sq, 1)

            def exps(h):
                act.wait_ge(s_sx, h + 1)
                mx = st[:, 32 + 4 * (h % 2):36 + 4 * (h % 2)]
                sm = st[:, 40 + 4 * (h % 2):44 + 4 * (h % 2)]
                for c in range(2):
                    for i in range(2):
                        keys = slice(0, 128) if i == 0 else slice(128, 384)
                        act.activation(sx[:, h % 2, c, keys], sx[:, h % 2, c, keys], ACT.Exp,
                                       bias=mx[:, 2 * c + i:2 * c + i + 1], scale=0.125,
                                       accum_out=sm[:, 2 * c + i:2 * c + i + 1]).then_inc(s_e, 1)

            def take_head(h):
                act.wait_ge(s_pt, h + 1)
                act.activation(pdT[:, h % 2], ps[:, h % 2, 0:384].rearrange("p (a k) -> p a k", k=P),
                               ACT.Copy).then_inc(s_ptc, 1)
                act.wait_ge(s_o, h + 1)
                act.activation(att[:, :, h, :], ps[:, 2 + h % 2, 0:256].rearrange("p (i d) -> p i d", d=P),
                               ACT.Copy).then_inc(s_oc, 1)

            for h in range(HEADS + 1):
                if h < HEADS:
                    exps(h)
                if h >= 1:
                    take_head(h - 1)
            act.wait_ge(s_ms, 1)
            act.activation(st[:, 64:80], st[:, 48:64], ACT.Sqrt).then_inc(s_rt, 1)

            act.wait_ge(s_lru, 1)
            act.activation(aT_hi[:, 8:16, :], xc, ACT.Copy).then_inc(s_lruhi, 1)
            for n in range(4):
                act.wait_ge(s_mt, n + 1)
                act.activation(aT_hi[:, 2 * n:2 * n + 2, :], ps4(4 + n), ACT.Copy).then_inc(s_mhi, 1)

            with act.Fori(OUT0, OUT0 + NB_OUT) as B:
                for s in range(SLABS):
                    split_hi(B, s)
            split_hi(WQ0, 0)

            norm_scalar(act, 0)

            for n in range(8):
                act.wait_ge(s_mt, 5 + n)
                act.activation(aT_hi[:, 2 * n:2 * n + 2, :], ps4(4 + n % 4), ACT.Copy).then_inc(s_mhi, 1)

            def take_pq(b):
                act.wait_ge(slab_used, 4 * (WQ0 + 1) + 4 * b)
                act.activation(arena[:, bass.ds(b * (TILES * COLS), TILES * COLS)]
                               .rearrange("p (i n) -> p i n", n=COLS), pair(b % 2), ACT.Copy).then_inc(banks_free, 1)

            for s in range(1, SLABS):
                split_hi(WQ0, s)
            with act.Fori(1, NB_WQ) as b:
                split_hi(b + WQ0, 0)
                split_hi(b + WQ0, 1)
                take_pq(b - 1)
                split_hi(b + WQ0, 2)
                split_hi(b + WQ0, 3)
            take_pq(NB_WQ - 1)
            for n in range(8):
                if n % 2 == 0:
                    act.wait_ge(s_qt, n + 1)
                    act.activation(pqT[:, 2 * n:2 * n + 2, :], ps4(4 + n % 4), ACT.Copy).then_inc(s_qtc[0], 1)
            for n in range(8):
                if n % 2 == 0:
                    act.wait_ge(s_scp, n + 1)
                    act.activation(sc_bank(n), ps[:, n % 4, :], ACT.Copy).then_inc(s_scc[0], 1)

            def gelu(j):
                act.wait_ge(slab_used, 4 * (U0 + 1) + 4 * j)
                act.activation(gs, pair(j % 2), ACT.Gelu_apprx_tanh).then_inc(banks_free, 1)
            for s in range(SLABS):
                split_hi(U0, s)

            def u_block(j):
                split_hi(j + U0, 0)
                split_hi(j + U0, 1)
                gelu(j - 1)
                split_hi(j + U0, 2)
                split_hi(j + U0, 3)
            with act.Fori(1, ROUTE) as j:
                u_block(j)
            act.wait_ge(s_gm, 1)
            act.activation(gate_exp, gate_exp, ACT.Exp).then_inc(s_ge, 1)
            with act.Fori(ROUTE, GATE_BLOCK) as j:
                u_block(j)

            def take_gates(m, t0, bank, gates):
                act.wait_ge(s_G, m + 1)
                act.activation(gates[:, :, bass.ds(t0, 4)].rearrange("p i t -> p t i"),
                               ps[:, bank, :].rearrange("p (t i) -> p t i", i=P), ACT.Copy).then_inc(s_Gc, 1)

            def gate_block(j, first=0):
                for s in range(SLABS):
                    split_hi(j + U0, s)
                    if s == 1:
                        gelu(j - 1)
                    if s >= first:
                        m = SLABS * j + (s - 2 - SLABS * GATE_BLOCK)
                        take_gates(m, 4 * m, 6 + s % 2, gates_late)
            gate_block(GATE_BLOCK, first=2)
            with act.Fori(GATE_BLOCK + 1, NB_U) as j:
                gate_block(j)
            split_hi(V0, 0)
            take_gates(LATE_BATCHES - 2, LATE - 8, 6, gates_late)
            gelu(NB_U - 1)
            take_gates(LATE_BATCHES - 1, LATE - 4, 7, gates_late)
            split_hi(V0, 1)
            act.wait_ge(s_ht, NB_U)
            with act.Fori(0, (BATCHES - LATE_BATCHES) // 4) as g:
                for k in range(4):
                    take_gates(4 * g + (LATE_BATCHES + k), 16 * g + 4 * k, 6 + k % 2, gates_early)

            def w_hi(b, s):
                act.wait_ge(s_w, 4 * b + s + 1)
                act.activation(wT_hi[:, s % 2, :], w_f(s), ACT.Copy).then_inc(s_whi, 1)

            def v_block(b, first=0):
                for s in range(SLABS):
                    if s >= first:
                        split_hi(b + V0, s)
                    w_hi(b, s)
            v_block(0, first=2)
            with act.Fori(1, NB_V) as b:
                v_block(b)
            norm_scalar(act, 2)

        @block.vector
        def _(dv):
            done = [0]

            def link(ins):
                done[0] += 1
                ins.then_inc(s_dv, 1)
                dv.wait_ge(s_dv, done[0])

            def split_lo(B, s):
                dv.wait_ge(hi_ready, 4 * B + (s + 1))
                dv.tensor_tensor(lo[:, s % 2], raw[:, s, :].rearrange("p (c n) -> p c n", n=COLS),
                                 hi[:, s % 2].bitcast(f32), ALU.subtract).then_inc(lo_ready, 1)

            dv.nop().then_inc(banks_free, 2)
            for s in range(SLABS):
                piece = slice(4 * s, 4 * s + 4)
                dv.wait_ge(s_xhi, s + 1)
                dv.tensor_tensor(aT_lo[:, piece, :], xs[:, piece, :], aT_hi[:, piece, :].bitcast(f32),
                                 ALU.subtract).then_inc(s_xlo, 1)
                split_lo(IN0, s)
            with dv.Fori(1, NB_IN) as b:
                for s in range(SLABS):
                    split_lo(b, s)

            dv.wait_ge(s_par, 48)
            link(dv.tensor_tensor(st[:, 192:320].rearrange("p (a d) -> p a d", d=QK_DIM),
                                  lamv[:, 0:4:2, :], lamv[:, 1:4:2, :], ALU.mult))
            dv.tensor_reduce(st[:, 128:130], st[:, 192:320].rearrange("p (a d) -> p a d", d=QK_DIM),
                             axis=AX.X, op=ALU.add).then_inc(s_lsum, 1)
            lam8, neg8 = par[:, 56:64], st[:, 0:8]
            link(dv.tensor_scalar(neg8, lam8, -1.0, None, ALU.mult))
            dv.tensor_tensor(neg8, neg8, lam8, ALU.min).then_inc(s_sp, 1)
            dv.wait_ge(s_u, 1)
            u8, r8, t8, q8 = st[:, 8:16], st[:, 80:88], st[:, 88:96], st[:, 96:104]
            link(dv.tensor_scalar(t8, u8, 2.0, None, ALU.add))
            link(dv.reciprocal(t8, t8))
            link(dv.tensor_tensor(r8, u8, t8, ALU.mult))
            link(dv.tensor_tensor(t8, r8, r8, ALU.mult))
            link(dv.memset(q8, 1.0 / 19))
            for n in range(8, -1, -1):
                link(dv.tensor_tensor(q8, q8, t8, ALU.mult))
                link(dv.tensor_scalar(q8, q8, 1.0 / (2 * n + 1), None, ALU.add))
            link(dv.tensor_tensor(q8, q8, r8, ALU.mult))
            link(dv.tensor_scalar(t8, lam8, -1.0, 0.0, ALU.mult, ALU.max))
            link(dv.scalar_tensor_tensor(q8, q8, 2.0, t8, ALU.mult, ALU.add))
            dv.tensor_scalar(st[:, 16:24], q8, 4.0, None, ALU.mult).then_inc(s_sp, 1)
            dv.wait_ge(s_lexp, 1)
            link(dv.tensor_tensor(st[:, 132:133], st[:, 131:132], st[:, 130:131], ALU.subtract))
            link(dv.tensor_scalar(st[:, 133:134], st[:, 132:133], -LAMBDA_INIT, None, ALU.add))

            for n in range(16):
                if n % 2 == 1:
                    dv.wait_ge(s_tr, n + 1)
                    dv.tensor_copy(front_target(n), ps4(4 + n % 4)).then_inc(s_trc[1], 1)
            link(dv.memset(xrT[:, :, 0:PAD], 0.0))
            dv.wait_ge(s_trc[0], 8)
            dv.wait_ge(s_trc[1], 8)
            for c in range(LRU_CHUNKS):
                link(dv.tensor_scalar(xc[:, c, :], xrT[:, c, 0:SEQ], conv_w(0, c), conv_b(c), ALU.mult, ALU.add))
                for j in (1, 2):
                    link(dv.scalar_tensor_tensor(xc[:, c, :], xrT[:, c, j:j + SEQ], conv_w(j, c), xc[:, c, :],
                                                 ALU.mult, ALU.add))
                dv.scalar_tensor_tensor(xc[:, c, :], xrT[:, c, 3:3 + SEQ], conv_w(3, c), xc[:, c, :],
                                        ALU.mult, ALU.add).then_inc(s_cp, 1)

            dv.wait_ge(s_cp, LRU_CHUNKS)
            dv.wait_ge(s_tanh, LRU_CHUNKS)
            dv.tensor_scalar(sq, th, 2.0 ** -116, None, ALU.max).then_inc(s_t2, 1)
            link(dv.tensor_scalar(rc, th, 1.0, None, ALU.add))
            link(dv.reciprocal(rc, rc))
            link(dv.tensor_scalar(th, th, -1.0, 1.0, ALU.mult, ALU.add))
            link(dv.tensor_tensor(th, th, rc, ALU.mult))
            link(dv.tensor_tensor(ig, ig, xc, ALU.mult))
            dv.wait_ge(s_sq, 1)
            link(dv.scalar_tensor_tensor(rc, sq, 2.0, rc, ALU.mult, ALU.mult))
            link(dv.tensor_tensor(ig, ig, rc, ALU.mult))
            for c in range(LRU_CHUNKS):
                last = dv.tensor_tensor_scan(rc[:, c, :], th[:, c, :], ig[:, c, :], 0.0, ALU.mult, ALU.add)
            link(last)
            dv.wait_ge(s_gx, 1)
            dv.tensor_tensor(xc, rc, xgT, ALU.mult).then_inc(s_lru, 1)

            def biased(h):
                dv.wait_ge(s_sc, h + 1)
                slope = 8.0 * 2.0 ** -(h + 1)
                link(dv.scalar_tensor_tensor(sx[:, h % 2], dist.unsqueeze(1).to_broadcast([P, 2, 384]), slope,
                                             ps[:, 4 + 2 * (h % 2):6 + 2 * (h % 2), 0:384], ALU.mult, ALU.add))
                mx = st[:, 32 + 4 * (h % 2):36 + 4 * (h % 2)].rearrange("p (c i) -> p c i", i=2)
                dv.tensor_reduce(mx[:, :, 0], sx[:, h % 2, :, 0:128], axis=AX.X, op=ALU.max)
                link(dv.tensor_reduce(mx[:, :, 1], sx[:, h % 2, :, 128:384], axis=AX.X, op=ALU.max))
                dv.tensor_scalar(st[:, 32 + 4 * (h % 2):36 + 4 * (h % 2)], st[:, 32 + 4 * (h % 2):36 + 4 * (h % 2)],
                                 -0.125, None, ALU.mult).then_inc(s_sx, 1)

            def mixed(h):
                dv.wait_ge(s_e, 4 * h + 4)
                sm = st[:, 40 + 4 * (h % 2):44 + 4 * (h % 2)]
                link(dv.reciprocal(sm, sm))
                link(dv.tensor_scalar(sm[:, 2:4], sm[:, 2:4], st[:, 133:134], None, ALU.mult))
                for i, keys in ((0, slice(0, 128)), (1, slice(128, 384))):
                    last = dv.tensor_scalar(sx[:, h % 2, 1, keys], sx[:, h % 2, 1, keys], sm[:, 2 + i:3 + i], None, ALU.mult)
                link(last)
                for i, keys in ((0, slice(0, 128)), (1, slice(128, 384))):
                    dv.scalar_tensor_tensor(sx[:, h % 2, 0, keys], sx[:, h % 2, 0, keys], sm[:, i:i + 1],
                                            sx[:, h % 2, 1, keys], ALU.mult, ALU.add).then_inc(s_pd, 1)

            for h in range(HEADS + 1):
                if h < HEADS:
                    if h >= 2:
                        dv.wait_ge(s_pt, h - 1)
                    biased(h)
                if h >= 1:
                    mixed(h - 1)
            dv.wait_ge(s_oc, HEADS)
            flat = at(20480, TILES * HEADS, P)
            ssq = at(4096, TILES * HEADS, P)
            link(dv.tensor_tensor(ssq, flat, flat, ALU.mult))
            link(dv.tensor_reduce(st[:, 48:64], ssq, axis=AX.X, op=ALU.add))
            dv.tensor_scalar(st[:, 48:64], st[:, 48:64], 1.0 / P, EPS, ALU.mult, ALU.add).then_inc(s_ms, 1)
            dv.wait_ge(s_rt, 1)
            newton(dv, link, st[:, 64:80], st[:, 48:64], st[:, 104:120])
            link(dv.tensor_scalar(st[:, 64:80], st[:, 64:80], 1.0 - LAMBDA_INIT, None, ALU.mult))
            link(dv.tensor_tensor(flat, flat, st[:, 64:80].unsqueeze(2).to_broadcast([P, 16, P]), ALU.mult))
            dv.tensor_tensor(flat, flat, subg.unsqueeze(1).to_broadcast([P, 16, P]), ALU.mult).then_inc(s_attn, 1)

            dv.wait_ge(s_lruhi, 1)
            dv.tensor_tensor(aT_lo[:, 8:16, :], xc, aT_hi[:, 8:16, :].bitcast(f32), ALU.subtract).then_inc(s_mlo, 1)

            def lo_from_psum(n, k, bank):
                dv.wait_ge(s_mhi, n + 1)
                dv.tensor_tensor(aT_lo[:, 2 * k:2 * k + 2, :], ps4(bank), aT_hi[:, 2 * k:2 * k + 2, :].bitcast(f32),
                                 ALU.subtract).then_inc(s_mlo, 1)
            for n in range(4):
                lo_from_psum(n, n, 4 + n)

            def take_mix(b):
                dv.wait_ge(slab_used, 4 * (OUT0 + 1) + 4 * b)
                dv.scalar_tensor_tensor(z_cols(4096, b), z_cols(14336, b), ALPHA, ps[:, bass.ds((b % 2) * 2, 2), :],
                                        ALU.mult, ALU.add).then_inc(banks_free, 1)

            def z_cols(off, b):
                return at(off, TILES, D_MODEL)[:, :, bass.ds(b * COLS, COLS)]

            for s in range(SLABS):
                split_lo(OUT0, s)
            dv.wait_ge(s_xn, 16)
            with dv.Fori(1, NB_OUT) as b:
                split_lo(b + OUT0, 0)
                split_lo(b + OUT0, 1)
                take_mix(b - 1)
                split_lo(b + OUT0, 2)
                split_lo(b + OUT0, 3)
            take_mix(NB_OUT - 1)
            dv.wait_ge(banks_free, 2 + NB_IN + NB_OUT)

            dv.wait_ge(s_ln1w, 32)
            for i in range(TILES):
                norm_stats(dv, link, 0, i, z[:, i, :])
            for i in range(TILES):
                norm_apply(dv, link, 0, i, z[:, i, :], lng, lnb, s_h)
            split_lo(WQ0, 0)
            for n in range(8):
                lo_from_psum(4 + n, n, 4 + n % 4)
            for s in range(1, SLABS):
                split_lo(WQ0, s)
            with dv.Fori(1, NB_WQ) as b:
                for s in range(SLABS):
                    split_lo(b + WQ0, s)
            for n in range(8):
                if n % 2 == 1:
                    dv.wait_ge(s_qt, n + 1)
                    dv.tensor_copy(pqT[:, 2 * n:2 * n + 2, :], ps4(4 + n % 4)).then_inc(s_qtc[1], 1)
            for n in range(8):
                if n % 2 == 1:
                    dv.wait_ge(s_scp, n + 1)
                    dv.tensor_copy(sc_bank(n), ps[:, n % 4, :]).then_inc(s_scc[1], 1)
            for taken in s_scc:
                dv.wait_ge(taken, 4)
            dv.nop().then_inc(s_htc, 1)

            dv.wait_ge(s_iota, 1)
            ROUTE_LINKS = 10

            def route(u, part):
                def link_route(n, ins):
                    ins.then_inc(s_route, 1)
                    dv.wait_ge(s_route, ROUTE_LINKS * u + n)
                    dv.sem_inc(s_pass, 1)
                if part == 0:
                    link_route(1, dv.tensor_copy(scu, sc_flat[:, bass.ds(u * (2 * P), 2 * P)]
                                                 .rearrange("p (a b) -> p a b", b=P)))
                    dv.max(m32[:, 0, 0:8], scu[:, 0, :])
                    link_route(2, dv.max(m32[:, 1, 0:8], scu[:, 1, :]))
                    for half in range(2):
                        dv.max_index(ix[:, half, 0:8], m32[:, half, 0:8], scu[:, half, :])
                elif part == 1:
                    dv.match_replace(rep[:, 0, :], m32[:, 0, 0:8], scu[:, 0, :], LOWEST)
                    link_route(3, dv.match_replace(rep[:, 1, :], m32[:, 1, 0:8], scu[:, 1, :], LOWEST))
                    dv.max(m32[:, 0, 8:16], rep[:, 0, :])
                    link_route(4, dv.max(m32[:, 1, 8:16], rep[:, 1, :]))
                    for half in range(2):
                        dv.max_index(ix[:, half, 8:16], m32[:, half, 8:16], rep[:, half, :])
                elif part == 2:
                    link_route(5, dv.tensor_tensor(cand.rearrange("p (a b) -> p a b", b=TOPK),
                                                   m32[:, 0, :].unsqueeze(2).to_broadcast([P, TOPK, TOPK]),
                                                   m32[:, 1, :].unsqueeze(1).to_broadcast([P, TOPK, TOPK]), ALU.add))
                    link_route(6, dv.max(top[:, 0:8], cand))
                    dv.max_index(topix[:, 0:8], top[:, 0:8], cand)
                    link_route(7, dv.match_replace(crep, top[:, 0:8], cand, LOWEST))
                else:
                    link_route(8, dv.max(top[:, 8:16], crep))
                    link_route(9, dv.max_index(topix[:, 8:16], top[:, 8:16], crep))
                    link_route(10, dv.tensor_copy(at_unit(u), found))

            def at_unit(u):
                return arena[:, bass.ds(FOUND + u * 64, 64)].bitcast(u32)

            def decode(n):
                if n == 0:
                    dv.tensor_scalar(places[:, 0], cand_ix, 4, None, ALU.logical_shift_right)
                    link(dv.tensor_scalar(places[:, 1], cand_ix, 15, None, ALU.bitwise_and))
                    dv.tensor_copy(places_f, places)
                    link(dv.tensor_copy(keys_f, key_ix))
                    return
                half, part, op = (n - 1) // 6, (n - 1) // 3 % 2, (n - 1) % 3
                units = slice(8 * part, 8 * part + 8)
                if op == 0:
                    link(dv.tensor_tensor(match, places_f[:, half, units, :].unsqueeze(3).to_broadcast([P, 8, TOPK, TOPK]),
                                          iota[:, 0:TOPK].unsqueeze(1).unsqueeze(1).to_broadcast([P, 8, TOPK, TOPK]),
                                          ALU.is_equal))
                elif op == 1:
                    link(dv.tensor_tensor(match, match, keys_f[:, units, half, :].unsqueeze(2)
                                          .to_broadcast([P, 8, TOPK, TOPK]), ALU.mult))
                else:
                    link(dv.tensor_reduce((key_a, key_b)[half][:, units, :], match, axis=AX.X, op=ALU.add))

            def take_gelu(j):
                dv.wait_ge(s_ht, j + 1)
                dv.tensor_copy(hT, ps[:, 4:6, :].rearrange("p a (c t) -> p (a c) t", t=SEQ)).then_inc(s_htc, 1)

            def u_block(j, side):
                for s in range(SLABS):
                    split_lo(j + U0, s)
                    if s == 1 and not (isinstance(j, int) and j == 0):
                        if not (isinstance(j, int) and j == 1):
                            dv.wait_ge(s_hts, 16 * j - 16)
                        take_gelu(j - 1)
                    side(s)

            for j in range(2):
                u_block(j, lambda s: route(j, s))
            with dv.Fori(2, ROUTE) as j:
                u_block(j, lambda s: route(j, s))
            dv.tensor_tensor(gate_exp, top_all, top_all[:, :, 0:1].to_broadcast([P, ROUTE, TOPK]),
                             ALU.subtract).then_inc(s_gm, 1)
            def finish_routing(n):
                if n < 13:
                    decode(n)
                elif n == 13:
                    dv.wait_ge(s_ge, 1)
                    link(dv.tensor_reduce(gsum, gate_exp, axis=AX.X, op=ALU.add))
                    link(dv.reciprocal(gsum, gsum))
                elif n == 14:
                    dv.tensor_tensor(gate_exp, gate_exp, gsum.unsqueeze(2).to_broadcast([P, ROUTE, TOPK]),
                                     ALU.mult).then_inc(s_gt, 1)
                elif n == 18:
                    dv.wait_ge(s_pk, 1)
                    for i in range(TILES):
                        dv.tensor_copy(picks[:, :, P * i:P * (i + 1)],
                                       ps[:, 6 + i, 0:384].rearrange("p (w t) -> p w t", w=3)).then_inc(s_pkc, 1)
                    dv.wait_ge(s_pkc, TILES)
            for j in range(ROUTE, GATE_BLOCK):
                u_block(j, lambda s: finish_routing(4 * (j - ROUTE) + s))

            def onehots(t0, view):
                dv.tensor_tensor(view, iota[:, :].unsqueeze(1).unsqueeze(1).to_broadcast([P, 2, 4, P]),
                                 picks[:, 0:2, bass.ds(t0, 4)].unsqueeze(3).to_broadcast([P, 2, 4, P]),
                                 ALU.is_equal).then_inc(s_oh0, 1)

            def late_onehots(j, s):
                m = SLABS * j + (s - SLABS * GATE_BLOCK)
                if not (isinstance(m, int) and m < 2):
                    dv.wait_ge(s_G, m - 1)
                onehots(4 * m + EARLY, hot_late[s % 2])

            u_block(GATE_BLOCK, lambda s: late_onehots(GATE_BLOCK, s))
            with dv.Fori(GATE_BLOCK + 1, NB_U) as j:
                u_block(j, lambda s: late_onehots(j, s))
            dv.wait_ge(s_G, LATE_BATCHES - 1)
            dv.wait_ge(lo_ready, 4 * V0)
            for k in range(4):
                onehots(4 * k, hot_early[k])
            split_lo(V0, 0)
            dv.wait_ge(s_hts, 16 * (NB_U - 1))
            take_gelu(NB_U - 1)
            with dv.Fori(1, (BATCHES - LATE_BATCHES) // 4) as g:
                for k in range(4):
                    dv.wait_ge(s_G, 4 * g + (LATE_BATCHES + k - 3))
                    onehots(16 * g + 4 * k, hot_early[k])
            split_lo(V0, 1)

            def product(b, s):
                n = 4 * b + s
                dv.wait_ge(s_hin[s // 2], 16 * b + 16)
                if not (isinstance(b, int) and n < 2):
                    dv.wait_ge(s_wlo, n - 1)
                for gates, tokens in ((gates_early, slice(0, EARLY)), (gates_late, slice(EARLY, SEQ))):
                    last = dv.tensor_tensor(w_f(s)[:, tokens], gates[:, bass.ds(n, 1), :].rearrange("p a t -> p (a t)"),
                                            hT[:, s, tokens], ALU.mult)
                last.then_inc(s_w, 1)

            def w_lo(b, s):
                dv.wait_ge(s_whi, 4 * b + s + 1)
                dv.tensor_tensor(wT_lo[:, s % 2, :], w_f(s), wT_hi[:, s % 2, :].bitcast(f32),
                                 ALU.subtract).then_inc(s_wlo, 1)

            def v_block(b, first=0, last=False):
                for s in range(SLABS):
                    if s < 3:
                        product(b, s + 1)
                    elif not last:
                        product(b + 1, 0)
                    if s >= first:
                        split_lo(b + V0, s)
                    w_lo(b, s)

            dv.wait_ge(s_Gc, BATCHES)
            product(0, 0)
            v_block(0, first=2)
            with dv.Fori(1, NB_V - 1) as b:
                v_block(b)
            v_block(NB_V - 1, last=True)

            dv.wait_ge(s_hre, 16)
            dv.wait_ge(slab_used, 4 * (V0 + NB_V))
            for i in range(TILES):
                link(dv.scalar_tensor_tensor(gates_z(i).rearrange("p (a n) -> p a n", n=COLS),
                                             h_back[:, i, :].rearrange("p (a n) -> p a n", n=COLS), ALPHA,
                                             ps[:, 4 * i:4 * i + 4, :], ALU.mult, ALU.add))
                norm_stats(dv, link, 2, i, gates_z(i))
            dv.wait_ge(s_ln2w, 32)
            for i in range(TILES):
                norm_apply(dv, link, 2, i, gates_z(i), lng2, lnb2, s_y, pieces=2)

        @block.tensor
        def _(pe):
            def block_products(B, par_, before=None, after=None):
                pe.wait_ge(banks_free, B + 1)
                for s in range(SLABS):
                    if before:
                        before(s)
                    for part in range(2):
                        pe.wait_ge((hi_ready, lo_ready)[part], 4 * B + (s + 1))
                        for c in range(4):
                            k = 4 * s + c
                            for i in range(TILES):
                                o = ps[:, bass.ds(par_ * 2 + i, 1), :].rearrange("p a n -> p (a n)")
                                t = slice(P * i, P * (i + 1))
                                if part == 0:
                                    pe.matmul(o, aT_hi[:, k, t], hi[:, s % 2, c], start=(k == 0), stop=False)
                                    pe.matmul(o, aT_lo[:, k, t], hi[:, s % 2, c], start=False, stop=False)
                                else:
                                    last = pe.matmul(o, aT_hi[:, k, t], lo[:, s % 2, c], start=False, stop=(k == 15))
                    last.then_inc(slab_used, 1)
                    if after:
                        after(s)

            with pe.Fori(0, NB_IN) as b:
                block_products(b, b % 2, before=lambda s: pe.wait_ge(s_xlo, s + 1))

            pe.wait_ge(s_const, 6)
            pe.wait_ge(banks_free, NB_IN + 2)
            for n in range(16):
                if n >= 4:
                    pe.wait_ge(s_trc[n % 2], (n - 4) // 2 + 1)
                kind, c0 = n // 4, 2 * (n % 4)
                first_block = (4, 6, 0, 2)[kind]
                for c in (c0, c0 + 1):
                    for i in range(TILES):
                        src = proj[:, first_block + c // 4, i, (c % 4) * P:(c % 4 + 1) * P]
                        last = pe.transpose(ps[:, 4 + n % 4, (2 * (c - c0) + i) * P:(2 * (c - c0) + i + 1) * P],
                                            src, ident)
                last.then_inc(s_tr, 1)

            for taken in s_trc:
                pe.wait_ge(taken, 8)
            for c in range(LRU_CHUNKS):
                pe.wait_ge(s_cp, c + 1)
                if c >= 4:
                    pe.wait_ge(s_sig, 2 * (c - 3))
                if c == 0:
                    pe.wait_ge(s_rg, 16)
                pe.matmul(ps[:, 4 + c % 4, 0:SEQ], rg_a(c), xc[:, c, :], start=True, stop=True)
                pe.matmul(ps[:, 4 + c % 4, SEQ:2 * SEQ], rg_x(c), xc[:, c, :], start=True, stop=True)\
                    .then_inc(s_gate, 1)

            def scores(h):
                if h < 2:
                    pe.wait_ge(s_sig, 16)
                else:
                    pe.wait_ge(s_sx, h - 1)
                for c in range(2):
                    rows = slice(QK_DIM * c, QK_DIM * (c + 1))
                    bank = 4 + 2 * (h % 2) + c
                    pe.matmul(ps[:, bank, 0:128], qT[rows, h, 0:128], kT[rows, h, 0:128], start=True, stop=True)
                    last = pe.matmul(ps[:, bank, 128:384], qT[rows, h, 128:256], kT[rows, h, :], start=True, stop=True)
                last.then_inc(s_sc, 1)

            def values(h):
                pe.wait_ge(s_pd, 2 * h + 2)
                if h >= 2:
                    pe.wait_ge(s_ptc, h - 1)
                for n, keys in enumerate((slice(0, 128), slice(128, 256), slice(256, 384))):
                    last = pe.transpose(ps[:, h % 2, P * n:P * (n + 1)], sx[:, h % 2, 0, keys], ident)
                last.then_inc(s_pt, 1)
                pe.wait_ge(s_ptc, h + 1)
                if h >= 2:
                    pe.wait_ge(s_oc, h - 1)

                def v_of(tile):
                    return proj[:, 8 + h // 4, tile, (h % 4) * P:(h % 4 + 1) * P]
                o = ps[:, 2 + h % 2, :]
                pe.matmul(o[:, 0:P], pdT[:, h % 2, 0, :], v_of(0), start=True, stop=True)
                pe.matmul(o[:, P:2 * P], pdT[:, h % 2, 1, :], v_of(0), start=True, stop=False)
                pe.matmul(o[:, P:2 * P], pdT[:, h % 2, 2, :], v_of(1), start=False, stop=True).then_inc(s_o, 1)

            for h in range(HEADS + 1):
                if h < HEADS:
                    scores(h)
                if h >= 1:
                    values(h - 1)

            pe.wait_ge(s_attn, 1)
            for n in range(4):
                for c in (2 * n, 2 * n + 1):
                    for i in range(TILES):
                        last = pe.transpose(ps[:, 4 + n, (2 * (c % 2) + i) * P:(2 * (c % 2) + i + 1) * P],
                                            att[:, i, c, :], ident)
                last.then_inc(s_mt, 1)

            pe.wait_ge(s_mlo, 5)
            with pe.Fori(0, NB_OUT) as b:
                block_products(b + OUT0, b % 2)

            pe.wait_ge(s_h, 2)
            for n in range(8):
                if n >= 4:
                    pe.wait_ge(s_mlo, 5 + n - 3)
                for c in (2 * n, 2 * n + 1):
                    for i in range(TILES):
                        last = pe.transpose(ps[:, 4 + n % 4, (2 * (c % 2) + i) * P:(2 * (c % 2) + i + 1) * P],
                                            z[:, i, P * c:P * (c + 1)], ident)
                last.then_inc(s_mt, 1)
            pe.wait_ge(s_mlo, 13)
            with pe.Fori(0, NB_WQ) as b:
                block_products(b + WQ0, b % 2)

            pe.wait_ge(banks_free, 2 + U0)
            for n in range(8):
                if n >= 4:
                    pe.wait_ge(s_qtc[n % 2], (n - 4) // 2 + 1)
                for c in (2 * n, 2 * n + 1):
                    for i in range(TILES):
                        last = pe.transpose(ps[:, 4 + n % 4, (2 * (c % 2) + i) * P:(2 * (c % 2) + i + 1) * P],
                                            pq[:, c // 4, i, (c % 4) * P:(c % 4 + 1) * P], ident)
                last.then_inc(s_qt, 1)
            for taken in s_qtc:
                pe.wait_ge(taken, 4)
            pe.wait_ge(s_sk, 16)
            for n in range(8):
                if n >= 4:
                    pe.wait_ge(s_scc[n % 2], (n - 4) // 2 + 1)
                i = n // 4
                for m in range(4):
                    hp = 4 * (n % 4) + m
                    last = pe.matmul(ps[:, n % 4, P * m:P * (m + 1)], pqT[:, hp, P * i:P * (i + 1)], skT[:, hp, :],
                                     start=True, stop=True)
                last.then_inc(s_scp, 1)
            for taken in s_scc:
                pe.wait_ge(taken, 4)

            def gelu_transposes(j):
                pe.wait_ge(banks_free, j + U0 + 3)
                pe.wait_ge(s_htc, j + 1)
                for c in range(4):
                    for i in range(TILES):
                        o = (2 * (c % 2) + i) * P
                        last = pe.transpose(ps[:, 4 + c // 2, o:o + P], gs[:, i, P * c:P * (c + 1)], ident)
                last.then_inc(s_ht, 1)

            block_products(U0, 0)
            def after_slab(j, s):
                if s == 0:
                    gelu_transposes(j - 1)
            with pe.Fori(1, GATE_BLOCK - 1) as j:
                block_products(j + U0, j % 2, after=lambda s: after_slab(j, s))

            def picks_transposes(s):
                after_slab(GATE_BLOCK - 1, s)
                if s == 0:
                    pe.wait_ge(s_gt, 1)
                    for i in range(TILES):
                        for w, src in enumerate((20736, 20992, 20480)):
                            last = pe.transpose(ps[:, 6 + i, P * w:P * (w + 1)], at(src + i * P, P), ident)
                    last.then_inc(s_pk, 1)
            block_products(GATE_BLOCK - 1 + U0, (GATE_BLOCK - 1) % 2, after=picks_transposes)

            def gate_products(m, bank, view):
                pe.wait_ge(s_oh, m + 1)
                if isinstance(m, int) and m < 2:
                    pe.wait_ge(s_pkc, TILES)
                else:
                    pe.wait_ge(s_Gc, m - 1)
                for t in range(4):
                    last = pe.matmul(ps[:, bank, P * t:P * (t + 1)], view[:, 1, t, :], view[:, 0, t, :],
                                     start=True, stop=True)
                last.then_inc(s_G, 1)

            def after_gate_slab(j, s):
                after_slab(j, s)
                gate_products(SLABS * j + (s - SLABS * GATE_BLOCK), 6 + s % 2, hot_late[s % 2])
            block_products(GATE_BLOCK + U0, GATE_BLOCK % 2, after=lambda s: after_gate_slab(GATE_BLOCK, s))
            with pe.Fori(GATE_BLOCK + 1, NB_U) as j:
                block_products(j + U0, j % 2, after=lambda s: after_gate_slab(j, s))
            for k in range(4):
                if k == 2:
                    gelu_transposes(NB_U - 1)
                gate_products(LATE_BATCHES + k, 6 + k % 2, hot_early[k])
            with pe.Fori(1, (BATCHES - LATE_BATCHES) // 4) as g:
                for k in range(4):
                    gate_products(4 * g + (LATE_BATCHES + k), 6 + k % 2, hot_early[k])

            def v_block(b, first=False, last=False):
                for s in range(SLABS):
                    n = 4 * b + s
                    start, stop = first and s == 0, last and s == 3
                    for part, (w, v) in enumerate(((wT_hi, hi), (wT_lo, hi), (wT_hi, lo))):
                        if part == 0:
                            pe.wait_ge(s_whi, n + 1)
                            pe.wait_ge(hi_ready, n + (4 * V0 + 1))
                        elif part == 1:
                            pe.wait_ge(s_wlo, n + 1)
                        else:
                            pe.wait_ge(lo_ready, n + (4 * V0 + 1))
                        for i in range(TILES):
                            for c in range(4):
                                done = pe.matmul(ps[:, 4 * i + c, :], w[:, s % 2, P * i:P * (i + 1)], v[:, s % 2, c],
                                                 start=start and part == 0, stop=stop and part == 2)
                    done.then_inc(slab_used, 1)
            pe.wait_ge(s_Gc, BATCHES)
            v_block(0, first=True)
            with pe.Fori(1, NB_V - 1) as b:
                v_block(b)
            v_block(NB_V - 1, last=True)


def kernel(**inputs):
    import concourse.bacc as bacc
    from concourse.bass_utils import run_bass_kernel_spmd as run

    a = {k: np.asarray(v) for k, v in inputs.items()}

    def blocks(w):
        n = w.shape[1] // 512
        return np.ascontiguousarray(w.reshape(4, 4, 128, n, 512).transpose(3, 0, 2, 1, 4)).reshape(n, 4, 128, 2048)

    x = a["x"][0]
    w_in = a["w_in"][0]
    q, k, v, xr, xg = (w_in[:, 1024 * n:1024 * (n + 1)] for n in range(5))
    col = lambda t: t.reshape(-1, 8, 128).transpose(2, 0, 1).reshape(128, -1)
    arrays = {
        "xT": x.T.reshape(16, 128, 256).transpose(1, 0, 2),
        "x": x,
        "w_in": blocks(np.concatenate([xr, xg, q, k, v], axis=1)),
        "w_out": blocks(a["w_out"][0]),
        "w_q": blocks(a["peer_wq"][0]),
        "uT": blocks(a["peer_u"][0].T),
        "v_tab": a["peer_v"][0].reshape(32, 4, 128, 2048),
        "subkeysT": a["peer_subkeys"][0].reshape(16, 128, 128).transpose(2, 0, 1),
        "params": np.concatenate([col(a["conv_w"][0]), col(a["conv_b"]), col(a["b_rg_a"].reshape(1, 1024)),
                                  col(a["b_rg_x"].reshape(1, 1024)), col(a["lru_lambda"])], axis=1),
        "lambdas": np.concatenate([a["lambda_q1"], a["lambda_k1"], a["lambda_q2"], a["lambda_k2"]], axis=0),
        "subln_g": a["subln_g"][0],
        "ln1_g": a["ln1_g"][0], "ln1_b": a["ln1_b"][0], "ln2_g": a["ln2_g"][0], "ln2_b": a["ln2_b"][0],
        "w_rg": np.stack([a["w_rg_a"][0], a["w_rg_x"][0]]).transpose(2, 0, 1, 3),
    }
    arrays = {n: np.ascontiguousarray(t) for n, t in arrays.items()}
    nc = bacc.Bacc("TRN2", target_bir_lowering=False, num_devices=1)
    f32 = mybir.dt.float32
    args = {n: nc.dram_tensor(n + "_dram", t.shape, f32, kind="ExternalInput").ap() for n, t in arrays.items()}
    out = nc.dram_tensor("out_dram", (1, 256, 2048), f32, kind="ExternalOutput").ap()
    gelu_dram = nc.dram_tensor("gelu_dram", (32, 128, 4, 256), f32, kind="Internal").ap()
    h_dram = nc.dram_tensor("h_dram", (256, 2048), f32, kind="Internal").ap()
    hybrid_layer(nc, **args, out=out, gelu_dram=gelu_dram, h_dram=h_dram)
    r = run(nc, [{n + "_dram": t for n, t in arrays.items()}], core_ids=[0])
    return r.results[0]["out_dram"]
```

```python
import math

import numpy as np

import concourse.bass as bass
from concourse import mybir
from contextlib import ExitStack


def hybrid_layer(nc, xT, x, w_in, w_out, w_q, uT, v_tab, subkeysT, params, lambdas, subln_g, w_rg,
                 ln1_g, ln1_b, ln2_g, ln2_b, out, gelu_dram, h_dram):
    f32, f32r, u32 = mybir.dt.float32, mybir.dt.float32r, mybir.dt.uint32
    ALU, ACT, AX = mybir.AluOpType, mybir.ActivationFunctionType, mybir.AxisListType

    P = 128
    D_MODEL = 2048
    SEQ = 256
    TILES = SEQ // P
    KC = D_MODEL // P
    COLS = 512
    SLABS = 4
    HEADS = 8
    QK_DIM = 64
    TOPK = 16
    LRU_CHUNKS = 8
    PAD = 3
    XROW = SEQ + PAD
    ALPHA = 2.0 ** 0.25
    EPS = 1e-5
    LAMBDA_INIT = 0.8 - 0.6 * math.exp(0.0)
    MASKED = -1e30
    LOWEST = -3.0e38

    IN0, OUT0, WQ0, U0, V0 = 0, 10, 14, 18, 50
    NB_IN, NB_OUT, NB_WQ, NB_U, NB_V = 10, 4, 4, 32, 32
    def takes(B):
        return 2 * B + (NB_IN + 2 * NB_OUT + 1 - 2 * (WQ0 + 1))
    ROUTE = TILES * HEADS

    ctx = ExitStack()
    with ctx:
        def sb(name, shape, dt=f32, stack=ctx):
            return stack.enter_context(nc.sbuf_tensor(name, shape, dt))

        def sem(name):
            return ctx.enter_context(nc.semaphore(name))

        raw = sb("raw", [P, SLABS, 2048])
        hi = sb("slab_hi", [P, 2, 4, COLS], f32r)
        lo = sb("slab_lo", [P, 2, 4, COLS], f32r)
        stage = sb("stage", [P, 2048])
        small = sb("small", [P, 768])
        picks_scope = ExitStack()
        picks = sb("picks", [P, 3, SEQ], stack=picks_scope)
        iota = sb("iota", [P, P], stack=picks_scope)
        picks_scope.close()
        wT_hi = sb("wT_hi", [P, 2, SEQ], f32r)
        wT_lo = sb("wT_lo", [P, 2, SEQ], f32r)
        front = ExitStack()
        aT = sb("aT", [P, KC, 2, SEQ], f32r, front)
        aT_hi, aT_lo = aT[:, :, 0, :], aT[:, :, 1, :]
        arena = sb("arena", [P, 24576], f32, front)
        front.close()
        gflat = sb("gates", [P, P * SEQ])
        ps = ctx.enter_context(nc.psum_tensor("ps", [P, 8, COLS], f32))

        def at(off, *dims):
            n = int(np.prod(dims))
            v = arena[:, off:off + n]
            if len(dims) == 1:
                return v
            names = "abcd"[:len(dims)]
            return v.rearrange(f"p ({' '.join(names)}) -> p {' '.join(names)}",
                               **{k: d for k, d in zip(names, dims)})

        xs = at(0, KC, SEQ)
        proj = at(4096, NB_IN, TILES, COLS)
        qT, kT = at(14336, HEADS, SEQ), at(16384, HEADS, SEQ)
        xgT = at(18432, LRU_CHUNKS, SEQ)
        xrT = at(20480, LRU_CHUNKS, XROW)
        xc, th = at(0, LRU_CHUNKS, SEQ), at(2048, LRU_CHUNKS, SEQ)
        ig, rc = at(4096, LRU_CHUNKS, SEQ), at(6144, LRU_CHUNKS, SEQ)
        att = at(20480, TILES, HEADS, P)
        sx = at(22528, 2, 384)
        pdT = at(23296, 3, P)
        par = at(23680, 64)
        lamv = at(23744, 4, QK_DIM)
        subg = at(24000, P)
        st = at(24128, 320)
        ident = small[:, 256:256 + P]
        dist = small[:, 384:768]
        squares = stage[:, 0:TILES * P]
        xn = at(0, TILES, D_MODEL)
        z = at(4096, TILES, D_MODEL)
        lng, lnb = at(8192, D_MODEL), at(10240, D_MODEL)
        pq = at(1024, TILES, COLS)
        pqT = at(8192, 2 * HEADS, SEQ)
        skT = at(12288, 2 * HEADS, P)
        sc = at(14336, TILES, 2 * HEADS * P)
        sc_flat = at(14336, TILES * 2 * HEADS * P)
        sT = at(0, 4, SEQ)

        conv_w = lambda j, c: par[:, 8 * j + c:8 * j + c + 1]
        conv_b = lambda c: par[:, 32 + c:33 + c]
        b_a = lambda c: par[:, 40 + c:41 + c]
        b_x = lambda c: par[:, 48 + c:49 + c]

        rg_a = lambda c: stage[:, P * c:P * (c + 1)]
        rg_x = lambda c: stage[:, 1024 + P * c:1024 + P * (c + 1)]
        hT = stage[:, 0:1024].rearrange("p (c t) -> p c t", t=SEQ)

        EARLY = 80
        LATE = SEQ - EARLY
        BATCHES, LATE_BATCHES = SEQ // 4, LATE // 4
        GATE_BLOCK = NB_U - LATE_BATCHES // SLABS
        gates_early = gflat[:, 0:P * EARLY].rearrange("p (i t) -> p i t", t=EARLY)
        gates_late = gflat[:, P * EARLY:].rearrange("p (i t) -> p i t", t=LATE)

        def hot(view):
            return view.rearrange("p (w t k) -> p w t k", w=2, t=4)
        hot_late = [hot(stage[:, 1024:2048]), hot(at(1024, 1024))]
        hot_early = [hot(stage[:, 1024:2048]), hot(raw[:, 2, 0:1024]), hot(raw[:, 2, 1024:2048]),
                     hot(raw[:, 3, 0:1024]), hot(raw[:, 3, 1024:2048])]
        EARLY_BANKS = (4, 5, 6, 7, 2)
        ROUND = len(hot_early)
        ROUNDS = (BATCHES - LATE_BATCHES) // ROUND

        LAST = P * EARLY
        h_back = gflat[:, LAST:LAST + 4096].rearrange("p (i d) -> p i d", d=D_MODEL)
        lng2, lnb2 = gflat[:, LAST + 4096:LAST + 6144], gflat[:, LAST + 6144:LAST + 8192]

        def gates_z(i):
            return gflat[:, LAST + 8192 + i * D_MODEL:LAST + 8192 + (i + 1) * D_MODEL]

        u_hi, u_lo = (t[:, :, :, :].rearrange("p s c n -> p s (c n)").rearrange("p s (c n) -> p s c n", n=SEQ)
                      for t in (hi, lo))

        def ps4(bank):
            return ps[:, bank, :].rearrange("p (c t) -> p c t", t=SEQ)

        def front_target(n):
            c = 2 * (n % 4)
            return xrT[:, c:c + 2, PAD:] if n < 4 else xgT[:, c:c + 2, :]

        def ps8(bank):
            return ps[:, bank:bank + 2, :].rearrange("p a (c t) -> p (a c) t", t=SEQ)

        SIDE0 = 4
        def scores_at(h): return 13 + 2 * h
        def ssq(g): return st[:, 48 + 8 * g:56 + 8 * g]
        def root(g): return st[:, 64 + 8 * g:72 + 8 * g]

        KEY_SCORES = (0, 1, 2, 4, 5, 6, 3, 7)

        def sc_bank(n):
            return sc[:, n // 4, (n % 4) * 512:(n % 4 + 1) * 512]

        def w_f(s):
            return small[:, 256 + (s % 2) * SEQ:256 + (s % 2 + 1) * SEQ]

        FOUND = 21504
        match = at(1024, 8, TOPK, TOPK)
        places = at(3072, 2, ROUTE, TOPK).bitcast(u32)
        places_f = at(3584, 2, ROUTE, TOPK)
        keys_f = at(4096, ROUTE, 2, TOPK)
        scu = at(18432, 2, P)
        rep = at(18688, 2, P)
        cand, crep = at(18944, 256), at(19200, 256)
        found = at(19456, 64).bitcast(u32)
        top, topix = at(19456, TOPK), at(19472, TOPK).bitcast(u32)
        ix = at(19488, 2, TOPK).bitcast(u32)
        m32 = at(19520, 2, TOPK)
        all_found = at(FOUND, ROUTE, 64)
        top_all = all_found[:, :, 0:16]
        cand_ix = all_found[:, :, 16:32].bitcast(u32)
        key_ix = all_found[:, :, 32:64].rearrange("p u (a k) -> p u a k", a=2).bitcast(u32)
        gate_exp = at(20480, ROUTE, TOPK)
        key_a = at(20736, ROUTE, TOPK)
        key_b = at(20992, ROUTE, TOPK)
        gsum = at(21248, ROUTE)

        def stat(i, base, a, n=1):
            o = 128 * (base // 2) + 64 * i + a
            return small[:, o:o + n]

        def both(a):
            return small[:, a:a + 65:64]

        loaded = [sem(f"slab_loaded_{s}") for s in range(SLABS)]
        hi_ready, lo_ready, slab_used = sem("hi_ready"), sem("lo_ready"), sem("slab_used")
        banks_free = sem("banks_free")
        const_ready, iota_ready, params_loaded = sem("const_ready"), sem("iota_ready"), sem("params_loaded")
        xT_loaded = [sem(f"xT_loaded_{s}") for s in range(SLABS)]
        x_hi_ready, x_lo_ready = sem("x_hi_ready"), sem("x_lo_ready")
        vector_chain = sem("vector_chain")
        rate_ready, rate_exp_done = sem("rate_ready"), sem("rate_exp_done")
        xr_xg_transposed, xr_xg_taken = sem("xr_xg_transposed"), sem("xr_xg_taken")
        conv_done, lru_gate_weights_loaded = sem("conv_done"), sem("lru_gate_weights_loaded")
        lru_gates_in_psum, sigmoids_done = sem("lru_gates_in_psum"), sem("sigmoids_done")
        decays_ready, tanhs_done, tanhs_clamped = sem("decays_ready"), sem("tanhs_done"), sem("tanhs_clamped")
        tanh_roots_done, lru_factor_ready = sem("tanh_roots_done"), sem("lru_factor_ready")
        lru_input_ready, lru_scanned = sem("lru_input_ready"), sem("lru_scanned")
        xg_gelu_done, lru_done = sem("xg_gelu_done"), sem("lru_done")
        lru_hi_ready, lru_lo_ready = sem("lru_hi_ready"), sem("lru_lo_ready")
        lambda_sums_ready, lambda_exps_done = sem("lambda_sums_ready"), sem("lambda_exps_done")
        qk_transposed, qk_taken = sem("qk_transposed"), [sem("qk_taken_by_dve"), sem("qk_taken_by_act")]
        scores_in_psum, scores_biased, exps_done = sem("scores_in_psum"), sem("scores_biased"), sem("exps_done")
        probs_ready, probs_transposed, probs_taken = sem("probs_ready"), sem("probs_transposed"), sem("probs_taken")
        att_in_psum, att_taken = sem("att_in_psum"), sem("att_taken")
        mean_squares_ready, att_roots_ready, att_normed = sem("mean_squares_ready"), sem("att_roots_ready"), sem("att_normed")
        mix_h_transposed, mix_h_hi_ready, mix_h_lo_ready = sem("mix_h_transposed"), sem("mix_h_hi_ready"), sem("mix_h_lo_ready")
        x_loaded, residual_ready, block_stats_ready = sem("x_loaded"), sem("residual_ready"), sem("block_stats_ready")
        ln1_weights_loaded, ln2_weights_loaded = sem("ln1_weights_loaded"), sem("ln2_weights_loaded")
        variance_ready, std_ready = sem("variance_ready"), sem("std_ready")
        h_ready, h_stored, h_reloaded = sem("h_ready"), sem("h_stored"), sem("h_reloaded")
        low_products_taken = sem("low_products_taken")
        queries_transposed, queries_taken = sem("queries_transposed"), sem("queries_taken")
        subkeys_loaded, key_scores_in_psum = sem("subkeys_loaded"), sem("key_scores_in_psum")
        key_scores_taken = [sem("key_scores_taken_by_act"), sem("key_scores_taken_by_dve")]
        route_chain, route_passed = sem("route_chain"), sem("route_passed")
        gate_logits_ready, gate_exps_done, gates_ready = sem("gate_logits_ready"), sem("gate_exps_done"), sem("gates_ready")
        picks_transposed, picks_ready = sem("picks_transposed"), sem("picks_ready")
        onehots_ready, onehots_weighed = sem("onehots_ready"), sem("onehots_weighed")
        gates_in_psum, gates_taken = sem("gates_in_psum"), sem("gates_taken")
        gelu_ready, gelu_stored = sem("gelu_ready"), sem("gelu_stored")
        first_gelu_loaded = [sem("first_gelu_loaded_0"), sem("first_gelu_loaded_1")]
        gelu_loaded = [sem("gelu_loaded_0"), sem("gelu_loaded_1")]
        w_ready, w_hi_ready, w_lo_ready = sem("w_ready"), sem("w_hi_ready"), sem("w_lo_ready")
        last_banks_done, y_ready, out_stored = sem("last_banks_done"), sem("y_ready"), sem("out_stored")

        block = ctx.enter_context(nc.Block())

        def newton(dv, link, root, var, tmp):
            link(dv.reciprocal(root, root))
            link(dv.tensor_tensor(tmp, root, root, ALU.mult))
            link(dv.tensor_tensor(tmp, tmp, var, ALU.mult))
            link(dv.tensor_scalar(tmp, tmp, -0.5, 1.5, ALU.mult, ALU.add))
            link(dv.tensor_tensor(root, root, tmp, ALU.mult))

        def variance(dv, link, base, i):
            link(dv.bn_aggr(stat(i, base, 24, 2), stat(i, base, 0, 24)))
            dv.tensor_scalar(stat(i, base, 26), stat(i, base, 25), EPS, None, ALU.add).then_inc(variance_ready, 1)

        @block.sync
        def _(sp):
            def stream(src, blocks, base, first=0):
                with sp.Fori(first, blocks) as b:
                    for s in range(SLABS):
                        sp.wait_ge(lo_ready, 4 * b + (4 * base + s - 3))
                        sp.dma_start(raw[:, s, :], src[b, s]).then_inc(loaded[s], 16)

            for s in range(SLABS):
                sp.dma_start(xs[:, 4 * s:4 * s + 4, :], xT[:, 4 * s:4 * s + 4, :]).then_inc(xT_loaded[s], 16)
                sp.dma_start(raw[:, s, :], w_in[0, s]).then_inc(loaded[s], 16)
            stream(w_in, NB_IN, IN0, first=1)
            stream(w_out, NB_OUT, OUT0)
            stream(w_q, NB_WQ, WQ0)
            stream(uT, NB_U, U0)
            for s in range(SLABS):
                if s == 2:
                    sp.wait_ge(gelu_stored, 16 * NB_U)
                    for half in range(2):
                        sp.dma_start(hT[:, 2 * half:2 * half + 2, :], gelu_dram[0, :, 2 * half:2 * half + 2, :])\
                            .then_inc(first_gelu_loaded[half], 16)
                    sp.wait_ge(gates_in_psum, BATCHES)
                sp.wait_ge(lo_ready, 4 * V0 + s - 3)
                sp.dma_start(raw[:, s, :], v_tab[0, s]).then_inc(loaded[s], 16)
            stream(v_tab, NB_V, V0, first=1)
            out_v = out.rearrange("b (i p) d -> p (b i) d", p=P)
            for n in range(2 * TILES):
                i, cols = n // 2, slice(1024 * (n % 2), 1024 * (n % 2) + 1024)
                sp.wait_ge(y_ready, n + 1)
                sp.dma_start(out_v[:, i, cols], gates_z(i)[:, cols]).then_inc(out_stored, 16)
            sp.wait_ge(out_stored, 16 * 2 * TILES)

        @block.gpsimd
        def _(pool):
            pool.memset(ident, 0.0).then_inc(const_ready, 1)
            pool.dma_start(stage[:, :].rearrange("p (w h j) -> p w h j", w=2, h=LRU_CHUNKS), w_rg).then_inc(lru_gate_weights_loaded, 16)
            pool.iota(dist[:, 0:128], [[1, 128]], base=0, channel_multiplier=-1,
                      allow_small_or_imprecise_dtypes=True).then_inc(const_ready, 1)
            pool.iota(dist[:, 128:384], [[1, 256]], base=-P, channel_multiplier=-1,
                      allow_small_or_imprecise_dtypes=True).then_inc(const_ready, 1)
            pool.iota(iota[:, :], [[1, P]], base=0, channel_multiplier=0,
                      allow_small_or_imprecise_dtypes=True).then_inc(iota_ready, 1)
            pool.wait_ge(const_ready, 3)
            pool.affine_select(out=ident, in_=ident, compare_op=ALU.not_equal, fill=1.0, base=0,
                               pattern=[[-1, P]], channel_multiplier=1).then_inc(const_ready, 1)
            pool.affine_select(out=dist[:, 0:128], in_=dist[:, 0:128], compare_op=ALU.is_ge, fill=MASKED,
                               base=0, pattern=[[-1, 128]], channel_multiplier=1).then_inc(const_ready, 1)
            pool.affine_select(out=dist[:, 128:384], in_=dist[:, 128:384], compare_op=ALU.is_ge, fill=MASKED,
                               base=P, pattern=[[-1, 256]], channel_multiplier=1).then_inc(const_ready, 1)
            pool.dma_start(par, params).then_inc(params_loaded, 16)
            pool.dma_start(lamv, lambdas.partition_broadcast(P)).then_inc(params_loaded, 16)
            pool.dma_start(subg, subln_g.partition_broadcast(P)).then_inc(params_loaded, 16)
            pool.wait_ge(sigmoids_done, 2 * LRU_CHUNKS)
            pool.tensor_tensor(ig, ig, xc, ALU.mult).then_inc(lru_input_ready, 1)
            pool.wait_ge(lru_factor_ready, 1)
            pool.wait_ge(lru_input_ready, 1)
            pool.tensor_tensor(ig, ig, th, ALU.mult).then_inc(lru_input_ready, 1)
            pool.wait_ge(lru_scanned, 3)
            pool.wait_ge(xg_gelu_done, 1)
            pool.tensor_tensor(xc, th, xgT, ALU.mult).then_inc(lru_done, 1)
            pool.wait_ge(lru_hi_ready, 1)
            pool.tensor_tensor(aT_lo[:, 0:8, :], xc, aT_hi[:, 0:8, :].bitcast(f32), ALU.subtract).then_inc(lru_lo_ready, 1)
            pool.wait_ge(lru_lo_ready, 1)
            pool.dma_start(xn, x.rearrange("(i p) d -> p i d", p=P)).then_inc(x_loaded, 16)
            pool.wait_ge(att_normed, 2)
            pool.wait_ge(mix_h_transposed, 2)
            pool.dma_start(lng, ln1_g.partition_broadcast(P)).then_inc(ln1_weights_loaded, 16)
            pool.dma_start(lnb, ln1_b.partition_broadcast(P)).then_inc(ln1_weights_loaded, 16)
            pool.dma_start(skT, subkeysT).then_inc(subkeys_loaded, 16)
            pool.wait_ge(h_ready, 4)
            pool.dma_start(h_dram.rearrange("(i p) d -> p i d", p=P), z).then_inc(h_stored, 16)
            pool.wait_ge(h_stored, 16)
            def store_gelu(j):
                pool.wait_ge(gelu_ready, 2 * j + 2)
                pool.dma_start(gelu_dram[j], hT).then_inc(gelu_stored, 16)

            def weigh(m, t0, view):
                pool.wait_ge(onehots_ready, m + 1)
                pool.tensor_tensor(view[:, 1], view[:, 1],
                                   picks[:, 2, bass.ds(t0, 4)].unsqueeze(2).to_broadcast([P, 4, P]), ALU.mult)\
                    .then_inc(onehots_weighed, 1)

            with pool.Fori(0, GATE_BLOCK - 1) as j:
                store_gelu(j)
            with pool.Fori(GATE_BLOCK, NB_U) as j:
                for s in range(SLABS):
                    m = SLABS * j + (s - SLABS * GATE_BLOCK)
                    weigh(m, 4 * m + EARLY, hot_late[s % 2])
                    if s == 1:
                        store_gelu(j - 1)
            for k in range(ROUND):
                weigh(LATE_BATCHES + k, 4 * k, hot_early[k])
            store_gelu(NB_U - 1)
            with pool.Fori(1, ROUNDS) as g:
                for k in range(ROUND):
                    weigh(ROUND * g + (LATE_BATCHES + k), 4 * ROUND * g + 4 * k, hot_early[k])
            with pool.Fori(1, NB_V) as b:
                for half in range(2):
                    pool.wait_ge(w_ready, 4 * b + (2 * half - 2))
                    pool.dma_start(hT[:, 2 * half:2 * half + 2, :], gelu_dram[b, :, 2 * half:2 * half + 2, :])\
                        .then_inc(gelu_loaded[half], 16)
            pool.dma_start(h_back, h_dram.rearrange("(i p) d -> p i d", p=P)).then_inc(h_reloaded, 16)
            pool.dma_start(lng2, ln2_g.partition_broadcast(P)).then_inc(ln2_weights_loaded, 16)
            pool.dma_start(lnb2, ln2_b.partition_broadcast(P)).then_inc(ln2_weights_loaded, 16)

        @block.scalar
        def _(act):
            def split_hi(B, s, reused=True):
                act.wait_ge(loaded[s], 16 * B + 16)
                if reused:
                    act.wait_ge(slab_used, 4 * B + (s - 1))
                act.activation(hi[:, s % 2], raw[:, s, :].rearrange("p (c n) -> p c n", n=COLS),
                               ACT.Copy).then_inc(hi_ready, 1)

            def pair(par_):
                return ps[:, bass.ds(par_ * 2, 2), :]

            for s in range(SLABS):
                piece = slice(4 * s, 4 * s + 4)
                act.wait_ge(xT_loaded[s], 16)
                act.activation(aT_hi[:, piece, :], xs[:, piece, :], ACT.Copy).then_inc(x_hi_ready, 1)
                split_hi(IN0, s, reused=s >= 2)

            def take_proj(b):
                act.wait_ge(slab_used, 4 * b + 4)
                act.activation(proj_block(b), pair(b % 2), ACT.Copy).then_inc(banks_free, 1)

            def proj_block(b):
                return arena[:, bass.ds(4096 + b * (TILES * COLS), TILES * COLS)]\
                    .rearrange("p (i n) -> p i n", n=COLS)

            with act.Fori(1, SIDE0) as b:
                split_hi(b, 0)
                split_hi(b, 1)
                take_proj(b - 1)
                split_hi(b, 2)
                split_hi(b, 3)

            def exps(h):
                act.wait_ge(scores_biased, h + 1)
                mx, sm = st[:, 32:36], st[:, 40:44]
                for c in range(2):
                    for i in range(2):
                        keys = slice(0, 128) if i == 0 else slice(128, 384)
                        act.activation(sx[:, c, keys], sx[:, c, keys], ACT.Exp, bias=mx[:, 2 * c + i:2 * c + i + 1],
                                       scale=0.125, accum_out=sm[:, 2 * c + i:2 * c + i + 1]).then_inc(exps_done, 1)

            def take_probs(h):
                act.wait_ge(probs_transposed, h + 1)
                act.activation(pdT, ps[:, 6, 0:384].rearrange("p (a k) -> p a k", k=P), ACT.Copy).then_inc(probs_taken, 1)

            def take_head(h):
                act.wait_ge(att_in_psum, h + 1)
                if h >= 1:
                    act.wait_ge(att_taken, 3 * h)
                act.activation(att[:, :, h, :], ps[:, 7, 0:256].rearrange("p (i d) -> p i d", d=P),
                               ACT.Copy).then_inc(att_taken, 1)
                for i in range(TILES):
                    o = 4 * i + h % 4
                    act.activation(squares[:, P * i:P * (i + 1)], ps[:, 7, P * i:P * (i + 1)], ACT.Square,
                                   accum_out=ssq(h // 4)[:, o:o + 1]).then_inc(att_taken, 1)

            def take_partial(n):
                act.wait_ge(slab_used, 4 * OUT0 + 2 * n + 2)
                act.activation(at(4096, TILES, D_MODEL)[:, :, n * COLS:(n + 1) * COLS], pair(n % 2),
                               ACT.Copy).then_inc(banks_free, 1)

            def side(k):
                if k % 4 == 1 and SIDE0 + k // 4 <= NB_IN:
                    take_proj(SIDE0 + k // 4 - 1)
                if k == 1:
                    act.wait_ge(rate_ready, 1)
                    act.activation(st[:, 8:16], st[:, 0:8], ACT.Exp).then_inc(rate_exp_done, 1)
                    act.wait_ge(lambda_sums_ready, 1)
                    act.activation(st[:, 130:132], st[:, 128:130], ACT.Exp).then_inc(lambda_exps_done, 1)
                if 2 <= k < 6:
                    for n in (2 * k - 4, 2 * k - 3):
                        act.wait_ge(xr_xg_transposed, n + 1)
                        act.activation(front_target(n), ps4(4 + n % 4), ACT.Copy).then_inc(xr_xg_taken, 1)
                if 6 <= k < 10:
                    for c in (2 * k - 12, 2 * k - 11):
                        act.wait_ge(lru_gates_in_psum, c + 1)
                        for gate, half, bias in ((th, 0, b_a), (ig, 1, b_x)):
                            act.activation(gate[:, c, :], ps[:, 4 + c % 4, SEQ * half:SEQ * (half + 1)], ACT.Sigmoid,
                                           bias=bias(c)).then_inc(sigmoids_done, 1)
                if 10 <= k < 12:
                    for c in range(4 * k - 40, 4 * k - 36):
                        act.wait_ge(sigmoids_done, 2 * LRU_CHUNKS)
                        act.wait_ge(rate_ready, 2)
                        act.activation(rc[:, c, :], th[:, c, :], ACT.Exp, scale=st[:, 24 + c:25 + c]).then_inc(decays_ready, 1)
                        act.wait_ge(decays_ready, c + 1)
                        act.activation(th[:, c, :], th[:, c, :], ACT.Tanh, scale=st[:, 16 + c:17 + c]).then_inc(tanhs_done, 1)
                if k == 12:
                    act.wait_ge(xr_xg_taken, 8)
                    act.activation(xgT, xgT, ACT.Gelu_apprx_tanh).then_inc(xg_gelu_done, 1)
                if k == 13:
                    act.wait_ge(tanhs_clamped, 1)
                    act.activation(th, th, ACT.Sqrt).then_inc(tanh_roots_done, 1)
                if k == 23:
                    act.wait_ge(lru_done, 1)
                    act.wait_ge(slab_used, 4 * SIDE0 + 22)
                    act.activation(aT_hi[:, 0:8, :], xc, ACT.Copy).then_inc(lru_hi_ready, 1)
                if k in (20, 22):
                    target = (qT, kT)[k // 2 - 10]
                    act.wait_ge(qk_transposed, k // 2 - 7)
                    act.activation(target[:, 4:8, :], ps8(4), ACT.Copy).then_inc(qk_taken[1], 1)
                h = k - scores_at(0)
                if 2 <= h < 2 + 2 * HEADS and h % 2 == 0:
                    exps(h // 2 - 1)
                if 4 <= h < 4 + 2 * HEADS and h % 2 == 0:
                    take_probs(h // 2 - 2)
                if k == 32:
                    mix_hi(0)
                if 5 <= h < 5 + 2 * HEADS and h % 2 == 1:
                    take_head(h // 2 - 2)
                if k in (30, 32):
                    act.wait_ge(mean_squares_ready, k // 2 - 14)
                    act.activation(root(k // 2 - 15), ssq(k // 2 - 15), ACT.Sqrt).then_inc(att_roots_ready, 1)
                if k >= 28 and k % 2 == 0:
                    take_partial(k // 2 - 14)
                if k == 33:
                    mix_hi(1)

            def mix_hi(g):
                act.wait_ge(mix_h_transposed, g + 1)
                act.activation(aT_hi[:, 8 + 4 * g:12 + 4 * g, :], ps8(4 + 2 * g), ACT.Copy).then_inc(mix_h_hi_ready, 1)

            for k in range(36):
                split_hi(SIDE0 + k // 4, k % 4)
                side(k)
            for s in range(SLABS):
                split_hi(OUT0 + 3, s)
            split_hi(WQ0, 0)

            act.wait_ge(variance_ready, 2)
            act.activation(both(27), both(26), ACT.Sqrt).then_inc(std_ready, 1)

            for s in range(SLABS):
                if s >= 1:
                    split_hi(WQ0, s)
                act.wait_ge(mix_h_transposed, 3 + s)
                act.activation(aT_hi[:, 4 * s:4 * s + 4, :], ps8(4 + 2 * (s % 2)), ACT.Copy).then_inc(mix_h_hi_ready, 1)

            def take_low(B, sub, sT_read=None):
                act.wait_ge(slab_used, 4 * B + (2 * sub + 2))
                if sT_read is None:
                    act.wait_ge(banks_free, takes(B) + (sub + 1))
                else:
                    act.wait_ge(gelu_ready, sT_read)
                banks, half = slice(2 - 2 * sub, 4 - 2 * sub), slice(2 * sub, 2 * sub + 2)
                act.activation(sT[:, half, :], ps[:, banks, SEQ:2 * SEQ], ACT.Copy).then_inc(low_products_taken, 1)

            def wq_block(B, first=False):
                for s in range(SLABS):
                    split_hi(B, s)
                    if s == 1 and first:
                        act.wait_ge(slab_used, 4 * (WQ0 + 1))
                        act.activation(pq, pair(0), ACT.Copy).then_inc(banks_free, 1)
                    elif s == 1:
                        take_low(B - 1, 1)
                    elif s == 3:
                        take_low(B, 0)
            wq_block(WQ0 + 1, first=True)
            with act.Fori(WQ0 + 2, U0) as B:
                wq_block(B)
            split_hi(U0, 0)
            take_low(U0 - 1, 1)
            for t in range(0, 8, 2):
                act.wait_ge(key_scores_in_psum, t + 1)
                act.activation(sc_bank(KEY_SCORES[t]), ps[:, 4 + t % 4, :], ACT.Copy).then_inc(key_scores_taken[0], 1)

            def gelu(j, sub):
                act.wait_ge(banks_free, takes(j + U0) + (3 + sub))
                if sub == 0 and not (isinstance(j, int) and j == 0):
                    act.wait_ge(gelu_stored, 16 * j)
                half = slice(2 * sub, 2 * sub + 2)
                act.activation(hT[:, half, :], sT[:, half, :], ACT.Gelu_apprx_tanh).then_inc(gelu_ready, 1)

            def u_slab(j, s):
                if not (isinstance(j, int) and j == 0 and s == 0):
                    split_hi(j + U0, s)
                if s == 3:
                    take_low(j + U0, 0, None if isinstance(j, int) and j == 0 else 2 * j - 1)
                elif not (isinstance(j, int) and j == 0):
                    if s == 1:
                        take_low(j + (U0 - 1), 1, None if isinstance(j, int) and j == 1 else 2 * j - 2)
                    else:
                        gelu(j - 1, s // 2)

            def u_block(j):
                for s in range(SLABS):
                    u_slab(j, s)
            u_block(0)
            u_block(1)
            with act.Fori(2, ROUTE) as j:
                u_block(j)
            act.wait_ge(gate_logits_ready, 1)
            act.activation(gate_exp, gate_exp, ACT.Exp).then_inc(gate_exps_done, 1)
            with act.Fori(ROUTE, GATE_BLOCK) as j:
                u_block(j)

            def take_gates(m, t0, bank, gates):
                act.wait_ge(gates_in_psum, m + 1)
                act.activation(gates[:, :, bass.ds(t0, 4)].rearrange("p i t -> p t i"),
                               ps[:, bank, :].rearrange("p (t i) -> p t i", i=P), ACT.Copy).then_inc(gates_taken, 1)

            def gate_block(j, first=0):
                for s in range(SLABS):
                    u_slab(j, s)
                    if s >= first:
                        m = SLABS * j + (s - 2 - SLABS * GATE_BLOCK)
                        take_gates(m, 4 * m, 6 + s % 2, gates_late)
            gate_block(GATE_BLOCK, first=2)
            with act.Fori(GATE_BLOCK + 1, NB_U) as j:
                gate_block(j)
            split_hi(V0, 0)
            take_gates(LATE_BATCHES - 2, LATE - 8, 6, gates_late)
            gelu(NB_U - 1, 0)
            take_low(U0 + NB_U - 1, 1, 2 * NB_U - 2)
            take_gates(LATE_BATCHES - 1, LATE - 4, 7, gates_late)
            gelu(NB_U - 1, 1)
            split_hi(V0, 1)
            act.wait_ge(gelu_ready, 2 * NB_U)
            with act.Fori(0, ROUNDS) as g:
                for k in range(ROUND):
                    take_gates(ROUND * g + (LATE_BATCHES + k), 4 * ROUND * g + 4 * k, EARLY_BANKS[k], gates_early)

            def w_hi(b, s):
                act.wait_ge(w_ready, 4 * b + s + 1)
                act.activation(wT_hi[:, s % 2, :], w_f(s), ACT.Copy).then_inc(w_hi_ready, 1)

            def v_block(b, first=0):
                for s in range(SLABS):
                    if s >= first:
                        split_hi(b + V0, s)
                    w_hi(b, s)
            v_block(0, first=2)
            with act.Fori(1, NB_V) as b:
                v_block(b)
            for i in range(TILES):
                act.wait_ge(variance_ready, TILES + i + 1)
                act.activation(stat(i, 2, 27), stat(i, 2, 26), ACT.Sqrt).then_inc(std_ready, 1)

        @block.vector
        def _(dv):
            done = [0]

            def link(ins):
                done[0] += 1
                ins.then_inc(vector_chain, 1)
                dv.wait_ge(vector_chain, done[0])

            def split_lo(B, s):
                dv.wait_ge(hi_ready, 4 * B + (s + 1))
                dv.tensor_tensor(lo[:, s % 2], raw[:, s, :].rearrange("p (c n) -> p c n", n=COLS),
                                 hi[:, s % 2].bitcast(f32), ALU.subtract).then_inc(lo_ready, 1)

            dv.nop().then_inc(banks_free, 2)
            for s in range(SLABS):
                piece = slice(4 * s, 4 * s + 4)
                dv.wait_ge(x_hi_ready, s + 1)
                dv.tensor_tensor(aT_lo[:, piece, :], xs[:, piece, :], aT_hi[:, piece, :].bitcast(f32),
                                 ALU.subtract).then_inc(x_lo_ready, 1)
                split_lo(IN0, s)
            with dv.Fori(1, SIDE0) as b:
                for s in range(SLABS):
                    split_lo(b, s)

            lam8, neg8 = par[:, 56:64], st[:, 0:8]
            u8, r8, t8, q8 = st[:, 8:16], st[:, 80:88], st[:, 88:96], st[:, 96:104]

            def lambda_and_rate_start():
                dv.wait_ge(params_loaded, 48)
                link(dv.tensor_tensor(st[:, 192:320].rearrange("p (a d) -> p a d", d=QK_DIM),
                                      lamv[:, 0:4:2, :], lamv[:, 1:4:2, :], ALU.mult))
                dv.tensor_reduce(st[:, 128:130], st[:, 192:320].rearrange("p (a d) -> p a d", d=QK_DIM),
                                 axis=AX.X, op=ALU.add).then_inc(lambda_sums_ready, 1)
                link(dv.tensor_scalar(neg8, lam8, -1.0, None, ALU.mult))
                dv.tensor_tensor(neg8, neg8, lam8, ALU.min).then_inc(rate_ready, 1)

            def rate():
                dv.wait_ge(rate_exp_done, 1)
                link(dv.tensor_scalar(t8, u8, 2.0, None, ALU.add))
                link(dv.reciprocal(t8, t8))
                link(dv.tensor_tensor(r8, u8, t8, ALU.mult))
                link(dv.tensor_tensor(t8, r8, r8, ALU.mult))
                link(dv.memset(q8, 1.0 / 19))
                for n in range(8, -1, -1):
                    link(dv.tensor_tensor(q8, q8, t8, ALU.mult))
                    link(dv.tensor_scalar(q8, q8, 1.0 / (2 * n + 1), None, ALU.add))
                link(dv.tensor_tensor(q8, q8, r8, ALU.mult))
                link(dv.tensor_scalar(t8, lam8, -1.0, 0.0, ALU.mult, ALU.max))
                link(dv.scalar_tensor_tensor(q8, q8, 2.0, t8, ALU.mult, ALU.add))
                dv.tensor_scalar(st[:, 24:32], q8, -8.0, None, ALU.mult)
                dv.tensor_scalar(st[:, 16:24], q8, 4.0, None, ALU.mult).then_inc(rate_ready, 1)

            def lambda_end():
                dv.wait_ge(lambda_exps_done, 1)
                link(dv.tensor_tensor(st[:, 132:133], st[:, 131:132], st[:, 130:131], ALU.subtract))
                link(dv.tensor_scalar(st[:, 133:134], st[:, 132:133], -LAMBDA_INIT, None, ALU.add))
                link(dv.memset(xrT[:, :, 0:PAD], 0.0))

            def conv(c):
                dv.wait_ge(xr_xg_taken, c // 2 + 1)
                link(dv.tensor_scalar(xc[:, c, :], xrT[:, c, 0:SEQ], conv_w(0, c), conv_b(c), ALU.mult, ALU.add))
                for j in (1, 2):
                    link(dv.scalar_tensor_tensor(xc[:, c, :], xrT[:, c, j:j + SEQ], conv_w(j, c), xc[:, c, :],
                                                 ALU.mult, ALU.add))
                dv.scalar_tensor_tensor(xc[:, c, :], xrT[:, c, 3:3 + SEQ], conv_w(3, c), xc[:, c, :],
                                        ALU.mult, ALU.add).then_inc(conv_done, 1)

            def scan(chunks):
                dv.wait_ge(lru_input_ready, 2)
                for c in chunks:
                    last = dv.tensor_tensor_scan(th[:, c, :], rc[:, c, :], ig[:, c, :], 0.0, ALU.mult, ALU.add)
                last.then_inc(lru_scanned, 1)

            def biased(h):
                dv.wait_ge(scores_in_psum, h + 1)
                if h == 0:
                    dv.wait_ge(conv_done, LRU_CHUNKS)
                else:
                    dv.wait_ge(probs_transposed, h)
                slope = 8.0 * 2.0 ** -(h + 1)
                link(dv.scalar_tensor_tensor(sx, dist.unsqueeze(1).to_broadcast([P, 2, 384]), slope,
                                             ps[:, 4:6, 0:384], ALU.mult, ALU.add))
                mx = st[:, 32:36].rearrange("p (c i) -> p c i", i=2)
                dv.tensor_reduce(mx[:, :, 0], sx[:, :, 0:128], axis=AX.X, op=ALU.max)
                link(dv.tensor_reduce(mx[:, :, 1], sx[:, :, 128:384], axis=AX.X, op=ALU.max))
                dv.tensor_scalar(st[:, 32:36], st[:, 32:36], -0.125, None, ALU.mult).then_inc(scores_biased, 1)

            def mixed(h):
                dv.wait_ge(exps_done, 4 * h + 4)
                sm = st[:, 40:44]
                link(dv.reciprocal(sm, sm))
                link(dv.tensor_scalar(sm[:, 2:4], sm[:, 2:4], st[:, 133:134], None, ALU.mult))
                for i, keys in ((0, slice(0, 128)), (1, slice(128, 384))):
                    last = dv.tensor_scalar(sx[:, 1, keys], sx[:, 1, keys], sm[:, 2 + i:3 + i], None, ALU.mult)
                link(last)
                for i, keys in ((0, slice(0, 128)), (1, slice(128, 384))):
                    dv.scalar_tensor_tensor(sx[:, 0, keys], sx[:, 0, keys], sm[:, i:i + 1],
                                            sx[:, 1, keys], ALU.mult, ALU.add).then_inc(probs_ready, 1)

            def mean_square(g):
                dv.wait_ge(att_taken, 12 * g + 12)
                dv.tensor_scalar(ssq(g), ssq(g), 1.0 / P, EPS, ALU.mult, ALU.add).then_inc(mean_squares_ready, 1)

            def rms_norm(g):
                dv.wait_ge(att_roots_ready, g + 1)
                newton(dv, link, root(g), ssq(g), st[:, 104:112])
                link(dv.tensor_scalar(root(g), root(g), 1.0 - LAMBDA_INIT, None, ALU.mult))
                for i in range(TILES):
                    for h in range(4):
                        o = att[:, i, 4 * g + h, :]
                        last = dv.scalar_tensor_tensor(o, o, root(g)[:, 4 * i + h:4 * i + h + 1], subg, ALU.mult, ALU.mult)
                last.then_inc(att_normed, 1)

            def mix_lo(g):
                dv.wait_ge(mix_h_hi_ready, g + 1)
                chunks = slice(8 + 4 * g, 12 + 4 * g)
                dv.tensor_tensor(aT_lo[:, chunks, :], ps8(4 + 2 * g), aT_hi[:, chunks, :].bitcast(f32),
                                 ALU.subtract).then_inc(mix_h_lo_ready, 1)

            def attention_side(k):
                h = k - scores_at(0)
                if 2 <= h < 2 + 2 * HEADS and h % 2 == 0:
                    biased(h // 2 - 1)
                if 3 <= h < 3 + 2 * HEADS and h % 2 == 1:
                    mixed(h // 2 - 1)

            def side(k):
                if k == 0:
                    lambda_and_rate_start()
                if k == 1:
                    rate()
                if k == 2:
                    lambda_end()
                if 3 <= k < 7:
                    conv(2 * k - 6)
                    conv(2 * k - 5)
                if k in (10, 11):
                    dv.wait_ge(qk_transposed, k - 9)
                    dv.tensor_copy((qT, kT)[k - 10][:, 0:4, :], ps8(4 + 2 * (k - 10))).then_inc(qk_taken[0], 1)
                if k == 12:
                    dv.wait_ge(tanhs_done, LRU_CHUNKS)
                    dv.tensor_scalar(th, th, 2.0 ** -116, None, ALU.max).then_inc(tanhs_clamped, 1)
                if k == 14:
                    dv.wait_ge(tanh_roots_done, 1)
                    dv.scalar_tensor_tensor(th, rc, 1.0, th, ALU.add, ALU.mult).then_inc(lru_factor_ready, 1)
                if 16 <= k < 19:
                    scan(range(3 * k - 48, min(3 * k - 45, LRU_CHUNKS)))
                if k == 28:
                    mean_square(0)
                if k == 31:
                    rms_norm(0)
                if k == 32:
                    mix_lo(0)
                    mean_square(1)
                    rms_norm(1)
                if k == 33:
                    mix_lo(1)

            def residual(n):
                dv.scalar_tensor_tensor(z_cols(4096, n), z_cols(0, n), ALPHA, z_cols(4096, n),
                                        ALU.mult, ALU.add).then_inc(residual_ready, 1)

            def take_mix(n):
                dv.wait_ge(slab_used, 4 * OUT0 + 2 * NB_OUT + 2 * n + 2)
                dv.wait_ge(residual_ready, n + 1)
                z_n = z_cols(4096, n)
                dv.tensor_tensor(z_n, z_n, pair(n % 2), ALU.add).then_inc(banks_free, 1)
                dv.wait_ge(banks_free, 3 + NB_IN + NB_OUT + n)
                for i in range(TILES):
                    dv.bn_stats(stat(i, 0, 6 * n, 6), z_n[:, i, :]).then_inc(block_stats_ready, 1)

            def pair(par_):
                return ps[:, bass.ds(par_ * 2, 2), :]

            def z_cols(off, b):
                return at(off, TILES, D_MODEL)[:, :, bass.ds(b * COLS, COLS)]

            for k in range(40):
                attention_side(k)
                split_lo(SIDE0 + k // 4, k % 4)
                side(k)
                if k == 35:
                    dv.wait_ge(x_loaded, 16)
                    dv.wait_ge(banks_free, 2 + NB_IN + NB_OUT)
                    residual(0)
                if k in (35, 37, 39):
                    take_mix(k // 2 - 17)
                if k in (36, 38):
                    residual(k // 2 - 17)
                if k == 38:
                    residual(3)
            split_lo(WQ0, 0)
            take_mix(NB_OUT - 1)
            dv.wait_ge(block_stats_ready, TILES * NB_OUT)
            for i in range(TILES):
                variance(dv, link, 0, i)
            dv.wait_ge(ln1_weights_loaded, 32)
            dv.wait_ge(std_ready, 1)
            newton(dv, link, both(27), both(26), both(28))
            for s in range(SLABS):
                cols = slice(COLS * s, COLS * (s + 1))
                for i in range(TILES):
                    last = dv.scalar_tensor_tensor(z[:, i, cols], z[:, i, cols], stat(i, 0, 24), lng[:, cols],
                                                   ALU.subtract, ALU.mult)
                link(last)
                for i in range(TILES):
                    last = dv.scalar_tensor_tensor(z[:, i, cols], z[:, i, cols], stat(i, 0, 27), lnb[:, cols],
                                                   ALU.mult, ALU.add)
                last.then_inc(h_ready, 1)
                if s >= 1:
                    split_lo(WQ0, s)
                dv.wait_ge(mix_h_hi_ready, 3 + s)
                dv.tensor_tensor(aT_lo[:, 4 * s:4 * s + 4, :], ps8(4 + 2 * (s % 2)),
                                 aT_hi[:, 4 * s:4 * s + 4, :].bitcast(f32), ALU.subtract).then_inc(mix_h_lo_ready, 1)

            def take_high(B, sub, target):
                dv.wait_ge(low_products_taken, 2 * B + (sub + 1 - 2 * (WQ0 + 1)))
                banks, half = slice(2 - 2 * sub, 4 - 2 * sub), slice(2 * sub, 2 * sub + 2)
                dv.tensor_tensor(target, ps[:, banks, 0:SEQ], sT[:, half, :], ALU.add).then_inc(banks_free, 1)

            def take_queries(B, sub):
                target = arena[:, bass.ds(B * (4 * SEQ) + (8192 + 2 * SEQ * sub - WQ0 * (4 * SEQ)), 2 * SEQ)]
                take_high(B, sub, target.rearrange("p (c t) -> p c t", t=SEQ))

            def wq_block(B, first=False):
                for s in range(SLABS):
                    split_lo(B, s)
                    if s == 1 and not first:
                        take_queries(B - 1, 1)
                    if s == 3:
                        take_queries(B, 0)
                        if first:
                            dv.wait_ge(queries_transposed, 1)
                            dv.tensor_copy(pqT[:, 0:4, :], ps8(4)).then_inc(queries_taken, 1)
            wq_block(WQ0 + 1, first=True)
            with dv.Fori(WQ0 + 2, U0) as B:
                wq_block(B)
            split_lo(U0, 0)
            take_queries(U0 - 1, 1)
            for t in range(1, 8, 2):
                dv.wait_ge(key_scores_in_psum, t + 1)
                dv.tensor_copy(sc_bank(KEY_SCORES[t]), ps[:, 4 + t % 4, :]).then_inc(key_scores_taken[1], 1)
            for taken in key_scores_taken:
                dv.wait_ge(taken, 4)

            dv.wait_ge(iota_ready, 1)
            ROUTE_LINKS = 10

            def route(u, part):
                def link_route(n, ins):
                    ins.then_inc(route_chain, 1)
                    dv.wait_ge(route_chain, ROUTE_LINKS * u + n)
                    dv.sem_inc(route_passed, 1)
                if part == 0:
                    link_route(1, dv.tensor_copy(scu, sc_flat[:, bass.ds(u * (2 * P), 2 * P)]
                                                 .rearrange("p (a b) -> p a b", b=P)))
                    dv.max(m32[:, 0, 0:8], scu[:, 0, :])
                    link_route(2, dv.max(m32[:, 1, 0:8], scu[:, 1, :]))
                    for half in range(2):
                        dv.max_index(ix[:, half, 0:8], m32[:, half, 0:8], scu[:, half, :])
                elif part == 1:
                    dv.match_replace(rep[:, 0, :], m32[:, 0, 0:8], scu[:, 0, :], LOWEST)
                    link_route(3, dv.match_replace(rep[:, 1, :], m32[:, 1, 0:8], scu[:, 1, :], LOWEST))
                    dv.max(m32[:, 0, 8:16], rep[:, 0, :])
                    link_route(4, dv.max(m32[:, 1, 8:16], rep[:, 1, :]))
                    for half in range(2):
                        dv.max_index(ix[:, half, 8:16], m32[:, half, 8:16], rep[:, half, :])
                elif part == 2:
                    link_route(5, dv.tensor_tensor(cand.rearrange("p (a b) -> p a b", b=TOPK),
                                                   m32[:, 0, :].unsqueeze(2).to_broadcast([P, TOPK, TOPK]),
                                                   m32[:, 1, :].unsqueeze(1).to_broadcast([P, TOPK, TOPK]), ALU.add))
                    link_route(6, dv.max(top[:, 0:8], cand))
                    dv.max_index(topix[:, 0:8], top[:, 0:8], cand)
                    link_route(7, dv.match_replace(crep, top[:, 0:8], cand, LOWEST))
                else:
                    link_route(8, dv.max(top[:, 8:16], crep))
                    link_route(9, dv.max_index(topix[:, 8:16], top[:, 8:16], crep))
                    link_route(10, dv.tensor_copy(at_unit(u), found))

            def at_unit(u):
                return arena[:, bass.ds(FOUND + u * 64, 64)].bitcast(u32)

            def decode(n):
                if n == 0:
                    dv.tensor_scalar(places[:, 0], cand_ix, 4, None, ALU.logical_shift_right)
                    link(dv.tensor_scalar(places[:, 1], cand_ix, 15, None, ALU.bitwise_and))
                    dv.tensor_copy(places_f, places)
                    link(dv.tensor_copy(keys_f, key_ix))
                    return
                half, part, op = (n - 1) // 6, (n - 1) // 3 % 2, (n - 1) % 3
                units = slice(8 * part, 8 * part + 8)
                if op == 0:
                    link(dv.tensor_tensor(match, places_f[:, half, units, :].unsqueeze(3).to_broadcast([P, 8, TOPK, TOPK]),
                                          iota[:, 0:TOPK].unsqueeze(1).unsqueeze(1).to_broadcast([P, 8, TOPK, TOPK]),
                                          ALU.is_equal))
                elif op == 1:
                    link(dv.tensor_tensor(match, match, keys_f[:, units, half, :].unsqueeze(2)
                                          .to_broadcast([P, 8, TOPK, TOPK]), ALU.mult))
                else:
                    link(dv.tensor_reduce((key_a, key_b)[half][:, units, :], match, axis=AX.X, op=ALU.add))

            def take_scores(j, sub):
                take_high(j + U0, sub, sT[:, 2 * sub:2 * sub + 2, :])

            def u_block(j, side):
                for s in range(SLABS):
                    if not (isinstance(j, int) and j == 0 and s == 0):
                        split_lo(j + U0, s)
                    if s == 1 and not (isinstance(j, int) and j == 0):
                        take_scores(j - 1, 1)
                    if s == 3:
                        take_scores(j, 0)
                    side(s)

            for j in range(2):
                u_block(j, lambda s: route(j, s))
            with dv.Fori(2, ROUTE) as j:
                u_block(j, lambda s: route(j, s))
            dv.tensor_tensor(gate_exp, top_all, top_all[:, :, 0:1].to_broadcast([P, ROUTE, TOPK]),
                             ALU.subtract).then_inc(gate_logits_ready, 1)
            def finish_routing(n):
                if n < 13:
                    decode(n)
                elif n == 13:
                    dv.wait_ge(gate_exps_done, 1)
                    link(dv.tensor_reduce(gsum, gate_exp, axis=AX.X, op=ALU.add))
                    link(dv.reciprocal(gsum, gsum))
                elif n == 14:
                    dv.tensor_tensor(gate_exp, gate_exp, gsum.unsqueeze(2).to_broadcast([P, ROUTE, TOPK]),
                                     ALU.mult).then_inc(gates_ready, 1)
                elif n == 18:
                    dv.wait_ge(picks_transposed, 1)
                    for i in range(TILES):
                        dv.tensor_copy(picks[:, :, P * i:P * (i + 1)],
                                       ps[:, 6 + i, 0:384].rearrange("p (w t) -> p w t", w=3)).then_inc(picks_ready, 1)
                    dv.wait_ge(picks_ready, TILES)
            for j in range(ROUTE, GATE_BLOCK):
                u_block(j, lambda s: finish_routing(4 * (j - ROUTE) + s))

            def onehots(t0, view):
                dv.tensor_tensor(view, iota[:, :].unsqueeze(1).unsqueeze(1).to_broadcast([P, 2, 4, P]),
                                 picks[:, 0:2, bass.ds(t0, 4)].unsqueeze(3).to_broadcast([P, 2, 4, P]),
                                 ALU.is_equal).then_inc(onehots_ready, 1)

            def late_onehots(j, s):
                m = SLABS * j + (s - SLABS * GATE_BLOCK)
                if not (isinstance(m, int) and m < 2):
                    dv.wait_ge(gates_in_psum, m - 1)
                onehots(4 * m + EARLY, hot_late[s % 2])

            u_block(GATE_BLOCK, lambda s: late_onehots(GATE_BLOCK, s))
            with dv.Fori(GATE_BLOCK + 1, NB_U) as j:
                u_block(j, lambda s: late_onehots(j, s))
            dv.wait_ge(gates_in_psum, LATE_BATCHES - 1)
            dv.wait_ge(lo_ready, 4 * V0)
            for k in range(ROUND):
                onehots(4 * k, hot_early[k])
            take_scores(NB_U - 1, 1)
            split_lo(V0, 0)
            with dv.Fori(1, ROUNDS) as g:
                for k in range(ROUND):
                    dv.wait_ge(gates_in_psum, ROUND * g + (LATE_BATCHES + k + 1 - ROUND))
                    onehots(4 * ROUND * g + 4 * k, hot_early[k])
            split_lo(V0, 1)

            def product(b, s):
                n = 4 * b + s
                if isinstance(b, int) and b == 0:
                    dv.wait_ge(first_gelu_loaded[s // 2], 16)
                else:
                    dv.wait_ge(gelu_loaded[s // 2], 16 * b)
                if not (isinstance(b, int) and n < 2):
                    dv.wait_ge(w_lo_ready, n - 1)
                for gates, tokens in ((gates_early, slice(0, EARLY)), (gates_late, slice(EARLY, SEQ))):
                    last = dv.tensor_tensor(w_f(s)[:, tokens], gates[:, bass.ds(n, 1), :].rearrange("p a t -> p (a t)"),
                                            hT[:, s, tokens], ALU.mult)
                last.then_inc(w_ready, 1)

            def w_lo(b, s):
                dv.wait_ge(w_hi_ready, 4 * b + s + 1)
                dv.tensor_tensor(wT_lo[:, s % 2, :], w_f(s), wT_hi[:, s % 2, :].bitcast(f32),
                                 ALU.subtract).then_inc(w_lo_ready, 1)

            def v_block(b, first=0, last=False):
                for s in range(SLABS):
                    if s < 3:
                        product(b, s + 1)
                    elif not last:
                        product(b + 1, 0)
                    if s >= first:
                        split_lo(b + V0, s)
                    w_lo(b, s)

            dv.wait_ge(gates_taken, BATCHES)
            product(0, 0)
            v_block(0, first=2)
            with dv.Fori(1, NB_V - 1) as b:
                v_block(b)
            v_block(NB_V - 1, last=True)

            dv.wait_ge(h_reloaded, 16)
            for i in range(TILES):
                for c in range(4):
                    cols = slice(COLS * c, COLS * (c + 1))
                    dv.wait_ge(last_banks_done, 4 * i + c + 1)
                    link(dv.scalar_tensor_tensor(gates_z(i)[:, cols], h_back[:, i, cols], ALPHA, ps[:, 4 * i + c, :],
                                                 ALU.mult, ALU.add))
                    last = dv.bn_stats(stat(i, 2, 6 * c, 6), gates_z(i)[:, cols])
                link(last)
                variance(dv, link, 2, i)
            dv.wait_ge(ln2_weights_loaded, 32)
            for i in range(TILES):
                zt = gates_z(i)
                dv.wait_ge(std_ready, 2 + i)
                newton(dv, link, stat(i, 2, 27), stat(i, 2, 26), stat(i, 2, 28))
                for half in range(2):
                    cols = slice(1024 * half, 1024 * (half + 1))
                    link(dv.scalar_tensor_tensor(zt[:, cols], zt[:, cols], stat(i, 2, 24), lng2[:, cols],
                                                 ALU.subtract, ALU.mult))
                    dv.scalar_tensor_tensor(zt[:, cols], zt[:, cols], stat(i, 2, 27), lnb2[:, cols],
                                            ALU.mult, ALU.add).then_inc(y_ready, 1)

        @block.tensor
        def _(pe):
            def slab_products(slab, s, k0, par_, start, stop, mid=None):
                for part in range(2):
                    pe.wait_ge((hi_ready, lo_ready)[part], slab + 1)
                    for c in range(4):
                        for i in range(TILES):
                            o = ps[:, bass.ds(par_ * 2 + i, 1), :].rearrange("p a n -> p (a n)")
                            k, t = k0 + c, slice(P * i, P * (i + 1))
                            if part == 0:
                                pe.matmul(o, aT_hi[:, k, t], hi[:, s % 2, c], start=start and c == 0, stop=False)
                                pe.matmul(o, aT_lo[:, k, t], hi[:, s % 2, c], start=False, stop=False)
                            else:
                                last = pe.matmul(o, aT_hi[:, k, t], lo[:, s % 2, c], start=False, stop=stop and c == 3)
                    if part == 0 and mid:
                        mid()
                last.then_inc(slab_used, 1)

            def block_products(B, par_, takes, before=None, after=None):
                pe.wait_ge(banks_free, takes + 1)
                for s in range(SLABS):
                    if before:
                        before(s)
                    slab_products(4 * B + s, s, 4 * s, par_, s == 0, s == 3)
                    if after:
                        after(s)

            with pe.Fori(0, SIDE0) as b:
                block_products(b, b % 2, b, before=lambda s: pe.wait_ge(x_lo_ready, s + 1))

            def transposes(n):
                pe.wait_ge(banks_free, 2 + 2 * (n // 4 + 1) if n % 4 >= 2 else 2 + 2 * (n // 4) + 1)
                if n >= 4:
                    pe.wait_ge(xr_xg_taken, n - 3)
                for c in (2 * (n % 4), 2 * (n % 4) + 1):
                    for i in range(TILES):
                        src = proj[:, 2 * (n // 4) + c // 4, i, (c % 4) * P:(c % 4 + 1) * P]
                        last = pe.transpose(ps[:, 4 + n % 4, (2 * (c % 2) + i) * P:(2 * (c % 2) + i + 1) * P], src, ident)
                last.then_inc(xr_xg_transposed, 1)

            def lru_gates(c):
                pe.wait_ge(conv_done, c + 1)
                pe.wait_ge(xr_xg_taken, min(8, 5 + c))
                if c >= 4:
                    pe.wait_ge(sigmoids_done, 2 * (c - 3))
                if c == 0:
                    pe.wait_ge(lru_gate_weights_loaded, 16)
                pe.matmul(ps[:, 4 + c % 4, 0:SEQ], rg_a(c), xc[:, c, :], start=True, stop=True)
                pe.matmul(ps[:, 4 + c % 4, SEQ:2 * SEQ], rg_x(c), xc[:, c, :], start=True, stop=True)\
                    .then_inc(lru_gates_in_psum, 1)

            def qk_transposes(block, bank):
                pe.wait_ge(banks_free, 2 + block + 1)
                for c in range(4):
                    for i in range(TILES):
                        o = (2 * (c % 2) + i) * P
                        last = pe.transpose(ps[:, bank + c // 2, o:o + P], proj[:, block, i, c * P:(c + 1) * P], ident)
                last.then_inc(qk_transposed, 1)

            def scores(h):
                if h == 0:
                    pe.wait_ge(qk_taken[0], 2)
                elif h == 3 or h == 4:
                    pe.wait_ge(qk_taken[1], h - 2)
                if h >= 1:
                    pe.wait_ge(scores_biased, h)
                for c in range(2):
                    rows = slice(QK_DIM * c, QK_DIM * (c + 1))
                    pe.matmul(ps[:, 4 + c, 0:128], qT[rows, h, 0:128], kT[rows, h, 0:128], start=True, stop=True)
                    last = pe.matmul(ps[:, 4 + c, 128:384], qT[rows, h, 128:256], kT[rows, h, :], start=True, stop=True)
                last.then_inc(scores_in_psum, 1)

            def probs_transposes(h):
                pe.wait_ge(probs_ready, 2 * h + 2)
                if h >= 1:
                    pe.wait_ge(probs_taken, h)
                for n, keys in enumerate((slice(0, 128), slice(128, 256), slice(256, 384))):
                    last = pe.transpose(ps[:, 6, P * n:P * (n + 1)], sx[:, 0, keys], ident)
                last.then_inc(probs_transposed, 1)

            def values(h):
                pe.wait_ge(probs_taken, h + 1)
                if h >= 1:
                    pe.wait_ge(att_taken, 3 * h)
                def v_of(tile):
                    return proj[:, 6 + 3 * (h // 4), tile, (h % 4) * P:(h % 4 + 1) * P]
                o = ps[:, 7, :]
                pe.matmul(o[:, 0:P], pdT[:, 0, :], v_of(0), start=True, stop=True)
                pe.matmul(o[:, P:2 * P], pdT[:, 1, :], v_of(0), start=True, stop=False)
                pe.matmul(o[:, P:2 * P], pdT[:, 2, :], v_of(1), start=False, stop=True).then_inc(att_in_psum, 1)

            def mix_transposes(g):
                pe.wait_ge(att_normed, g + 1)
                for c in range(4):
                    for i in range(TILES):
                        o = (2 * (c % 2) + i) * P
                        last = pe.transpose(ps[:, 4 + 2 * g + c // 2, o:o + P], att[:, i, 4 * g + c, :], ident)
                last.then_inc(mix_h_transposed, 1)

            def side(k):
                if k < 4:
                    transposes(2 * k)
                    transposes(2 * k + 1)
                if 4 <= k < 8:
                    lru_gates(2 * k - 8)
                    lru_gates(2 * k - 7)
                if k == 8:
                    pe.wait_ge(sigmoids_done, 12)
                    qk_transposes(4, 4)
                if k == 9:
                    pe.wait_ge(sigmoids_done, 16)
                    qk_transposes(5, 6)
                if k in (18, 20):
                    pe.wait_ge(scores_biased, k // 2 - 6)
                    qk_transposes(7 + k // 2 - 9, 4)
                h = k - scores_at(0)
                if 0 <= h < 2 * HEADS and h % 2 == 0:
                    scores(h // 2)
                if 2 <= h < 2 + 2 * HEADS and h % 2 == 0:
                    probs_transposes(h // 2 - 1)
                if 3 <= h < 3 + 2 * HEADS and h % 2 == 1:
                    values(h // 2 - 1)
                if k == 30:
                    mix_transposes(0)
                if k == 31:
                    pe.wait_ge(att_taken, 3 * HEADS)
                    mix_transposes(1)

            pe.wait_ge(const_ready, 6)
            for b in range(SIDE0, NB_IN):
                block_products(b, b % 2, b, after=lambda s: side(4 * (b - SIDE0) + s))
            pe.wait_ge(lru_lo_ready, 1)
            for n in range(NB_OUT):
                pe.wait_ge(banks_free, NB_IN + n + 1)
                for e in range(2):
                    slab = 4 * OUT0 + 2 * n + e
                    slab_products(slab, slab % 4, 4 * e, n % 2, e == 0, e == 1)
                    side(slab - 4 * SIDE0)
            for n in range(NB_OUT):
                pe.wait_ge(banks_free, NB_IN + NB_OUT + n + 1)
                for e in range(2):
                    if n == 0:
                        pe.wait_ge(mix_h_lo_ready, e + 1)
                    slab = 4 * OUT0 + 2 * NB_OUT + 2 * n + e
                    slab_products(slab, slab % 4, 8 + 4 * e, n % 2, e == 0, e == 1)

            def h_transposes(s):
                pe.wait_ge(h_ready, s + 1)
                if s >= 2:
                    pe.wait_ge(mix_h_lo_ready, 1 + s)
                for c in range(4):
                    for i in range(TILES):
                        o = (2 * (c % 2) + i) * P
                        last = pe.transpose(ps[:, 4 + 2 * (s % 2) + c // 2, o:o + P],
                                            z[:, i, P * (4 * s + c):P * (4 * s + c + 1)], ident)
                last.then_inc(mix_h_transposed, 1)

            h_transposes(0)
            pe.wait_ge(banks_free, WQ0 + NB_OUT + 1)
            for s in range(SLABS):
                pe.wait_ge(mix_h_lo_ready, 3 + s)
                slab_products(4 * WQ0 + s, s, 4 * s, 0, s == 0, s == 3,
                              mid=(lambda: h_transposes(s + 1)) if s < 3 else None)

            def transposed_block(B, after=None):
                for s in range(SLABS):
                    sub, e = s // 2, s % 2
                    if e == 0:
                        pe.wait_ge(banks_free, takes(B) + (1 + sub))
                    bank = 2 - 2 * sub
                    pe.wait_ge(hi_ready, 4 * B + (s + 1))
                    for c in range(8):
                        for x in range(2):
                            pe.matmul(ps[:, bank + x, :], u_hi[:, e, c, P * x:P * (x + 1)],
                                      aT[:, 8 * e + c].rearrange("p a t -> p (a t)"),
                                      start=(e == 0 and c == 0), stop=False)
                    pe.wait_ge(lo_ready, 4 * B + (s + 1))
                    for c in range(8):
                        for x in range(2):
                            last = pe.matmul(ps[:, bank + x, 0:SEQ], u_lo[:, e, c, P * x:P * (x + 1)],
                                             aT_hi[:, 8 * e + c], start=False, stop=(e == 1 and c == 7))
                    last.then_inc(slab_used, 1)
                    if after:
                        after(s)

            def query_transposes(s):
                if s == 1:
                    pe.wait_ge(banks_free, takes(WQ0 + 1) + 2)
                    for c in range(4):
                        for i in range(TILES):
                            o = (2 * (c % 2) + i) * P
                            last = pe.transpose(ps[:, 4 + c // 2, o:o + P], pq[:, i, c * P:(c + 1) * P], ident)
                    last.then_inc(queries_transposed, 1)
            transposed_block(WQ0 + 1, query_transposes)
            with pe.Fori(WQ0 + 2, U0) as B:
                transposed_block(B)

            pe.wait_ge(subkeys_loaded, 16)
            pe.wait_ge(queries_taken, 1)
            for t, n in enumerate(KEY_SCORES):
                pe.wait_ge(banks_free, takes(U0) + (2 if n % 4 == 3 else 0))
                if t >= 4:
                    pe.wait_ge(key_scores_taken[t % 2], (t - 4) // 2 + 1)
                for m in range(4):
                    hp = 4 * (n % 4) + m
                    last = pe.matmul(ps[:, 4 + t % 4, P * m:P * (m + 1)], pqT[:, hp, P * (n // 4):P * (n // 4 + 1)],
                                     skT[:, hp, :], start=True, stop=True)
                last.then_inc(key_scores_in_psum, 1)

            def u_block(j, after=None):
                transposed_block(j + U0, after)

            with pe.Fori(0, GATE_BLOCK - 1) as j:
                u_block(j)

            def picks_transposes(s):
                if s == 0:
                    pe.wait_ge(gates_ready, 1)
                    for i in range(TILES):
                        for w, src in enumerate((20736, 20992, 20480)):
                            last = pe.transpose(ps[:, 6 + i, P * w:P * (w + 1)], at(src + i * P, P), ident)
                    last.then_inc(picks_transposed, 1)
            for taken in key_scores_taken:
                pe.wait_ge(taken, 4)
            u_block(GATE_BLOCK - 1, picks_transposes)

            def gate_products(m, bank, view, taken):
                pe.wait_ge(onehots_weighed, m + 1)
                if taken is not None:
                    pe.wait_ge(gates_taken, taken)
                for t in range(4):
                    last = pe.matmul(ps[:, bank, P * t:P * (t + 1)], view[:, 1, t, :], view[:, 0, t, :],
                                     start=True, stop=True)
                last.then_inc(gates_in_psum, 1)

            def after_gate_slab(j, s):
                m = SLABS * j + (s - SLABS * GATE_BLOCK)
                if isinstance(m, int) and m < 2:
                    pe.wait_ge(picks_ready, TILES)
                gate_products(m, 6 + s % 2, hot_late[s % 2], None if isinstance(m, int) and m < 2 else m - 1)
            u_block(GATE_BLOCK, lambda s: after_gate_slab(GATE_BLOCK, s))
            with pe.Fori(GATE_BLOCK + 1, NB_U) as j:
                u_block(j, lambda s: after_gate_slab(j, s))
            for k in range(ROUND):
                if EARLY_BANKS[k] < 4:
                    pe.wait_ge(banks_free, takes(U0 + NB_U) + 1)
                gate_products(LATE_BATCHES + k, EARLY_BANKS[k], hot_early[k],
                              LATE_BATCHES + k - 3 if EARLY_BANKS[k] >= 6 else None)
            with pe.Fori(1, ROUNDS) as g:
                for k in range(ROUND):
                    gate_products(ROUND * g + (LATE_BATCHES + k), EARLY_BANKS[k], hot_early[k],
                                  ROUND * g + (LATE_BATCHES + k + 1 - ROUND))

            def v_block(b, first=False, last=False):
                for s in range(SLABS - 1 if last else SLABS):
                    n = 4 * b + s
                    start = first and s == 0
                    for part, (w, v) in enumerate(((wT_hi, hi), (wT_lo, hi), (wT_hi, lo))):
                        if part == 0:
                            pe.wait_ge(w_hi_ready, n + 1)
                            pe.wait_ge(hi_ready, n + (4 * V0 + 1))
                        elif part == 1:
                            pe.wait_ge(w_lo_ready, n + 1)
                        else:
                            pe.wait_ge(lo_ready, n + (4 * V0 + 1))
                        for i in range(TILES):
                            for c in range(4):
                                done = pe.matmul(ps[:, 4 * i + c, :], w[:, s % 2, P * i:P * (i + 1)], v[:, s % 2, c],
                                                 start=start and part == 0, stop=False)
                    done.then_inc(slab_used, 1)
            pe.wait_ge(gates_taken, BATCHES)
            v_block(0, first=True)
            with pe.Fori(1, NB_V - 1) as b:
                v_block(b)
            v_block(NB_V - 1, last=True)
            pe.wait_ge(w_lo_ready, 4 * NB_V)
            pe.wait_ge(lo_ready, 4 * (V0 + NB_V))
            for i in range(TILES):
                for c in range(4):
                    for w, v in ((wT_hi, hi), (wT_lo, hi), (wT_hi, lo)):
                        done = pe.matmul(ps[:, 4 * i + c, :], w[:, 1, P * i:P * (i + 1)], v[:, 1, c],
                                         start=False, stop=w is wT_hi and v is lo)
                    done.then_inc(last_banks_done, 1)


def kernel(**inputs):
    import concourse.bacc as bacc
    from concourse.bass_utils import run_bass_kernel_spmd as run

    a = {k: np.asarray(v) for k, v in inputs.items()}

    def blocks(w):
        n = w.shape[1] // 512
        return np.ascontiguousarray(w.reshape(4, 4, 128, n, 512).transpose(3, 0, 2, 1, 4)).reshape(n, 4, 128, 2048)

    def blocks_of_256(w):
        n = w.shape[1] // 512
        return w.reshape(2, 8, 128, 2 * n, 256).transpose(3, 0, 2, 1, 4).reshape(n, 4, 128, 2048)

    x = a["x"][0]
    w_in = a["w_in"][0]
    q, k, v, xr, xg = (w_in[:, 1024 * n:1024 * (n + 1)] for n in range(5))
    col = lambda t: t.reshape(-1, 8, 128).transpose(2, 0, 1).reshape(128, -1)
    arrays = {
        "xT": x.T.reshape(16, 128, 256).transpose(1, 0, 2),
        "x": x,
        "w_in": blocks(np.concatenate([xr, xg] + [t[:, 512 * n:512 * n + 512] for n in range(2) for t in (q, k, v)],
                                      axis=1)),
        "w_out": np.concatenate([blocks(a["w_out"][0])[:, n:n + 2].reshape(2, 4, 128, 2048) for n in (2, 0)]),
        "w_q": np.concatenate([blocks(a["peer_wq"][0][:, :512]), blocks_of_256(a["peer_wq"][0][:, 512:])]),
        "uT": blocks_of_256(a["peer_u"][0].T),
        "v_tab": a["peer_v"][0].reshape(32, 4, 128, 2048),
        "subkeysT": a["peer_subkeys"][0].reshape(16, 128, 128).transpose(2, 0, 1),
        "params": np.concatenate([col(a["conv_w"][0]), col(a["conv_b"]), col(a["b_rg_a"].reshape(1, 1024)),
                                  col(a["b_rg_x"].reshape(1, 1024)), col(a["lru_lambda"])], axis=1),
        "lambdas": np.concatenate([a["lambda_q1"], a["lambda_k1"], a["lambda_q2"], a["lambda_k2"]], axis=0),
        "subln_g": a["subln_g"][0],
        "ln1_g": a["ln1_g"][0], "ln1_b": a["ln1_b"][0], "ln2_g": a["ln2_g"][0], "ln2_b": a["ln2_b"][0],
        "w_rg": np.stack([a["w_rg_a"][0], a["w_rg_x"][0]]).transpose(2, 0, 1, 3),
    }
    arrays = {n: np.ascontiguousarray(t) for n, t in arrays.items()}
    nc = bacc.Bacc("TRN2", target_bir_lowering=False, num_devices=1)
    f32 = mybir.dt.float32
    args = {n: nc.dram_tensor(n + "_dram", t.shape, f32, kind="ExternalInput").ap() for n, t in arrays.items()}
    out = nc.dram_tensor("out_dram", (1, 256, 2048), f32, kind="ExternalOutput").ap()
    gelu_dram = nc.dram_tensor("gelu_dram", (32, 128, 4, 256), f32, kind="Internal").ap()
    h_dram = nc.dram_tensor("h_dram", (256, 2048), f32, kind="Internal").ap()
    hybrid_layer(nc, **args, out=out, gelu_dram=gelu_dram, h_dram=h_dram)
    r = run(nc, [{n + "_dram": t for n, t in arrays.items()}], core_ids=[0])
    return r.results[0]["out_dram"]
```
